# Optimizing a Trainium2 kernel written in Bass

```python
import jax, jax.numpy as jnp
from jax import lax
import numpy as np
import math

D_MODEL = 1024
BATCH = 1
SEQ = 1024
DEPTH = 1

MIX_WIDTH = D_MODEL
HEAD_DIM = 64
ATTN_WIDTH = MIX_WIDTH // 2
N_Q_HEADS = ATTN_WIDTH // HEAD_DIM
N_KV_HEADS = 2
KV_WIDTH = N_KV_HEADS * HEAD_DIM
TOK_WIDTH = MIX_WIDTH - ATTN_WIDTH
N_TOK_HEADS = TOK_WIDTH // HEAD_DIM
N_IN = ATTN_WIDTH + 2 * KV_WIDTH + 2 * TOK_WIDTH
CHUNK = 128
Q_BLOCK = 128
GRID_W = 64
ROPE_THETA = 10000.0
D_FF = 2816
CONV_W = 3
N_MOD = 6
EPS = 1e-6


def rmsnorm(x, g):
    xf = x.astype(jnp.float32)
    y = xf * lax.rsqrt(jnp.mean(xf * xf, axis=-1, keepdims=True) + EPS)
    return (y * g.astype(jnp.float32)).astype(x.dtype)

def axial_rope_tables(seq_len):
    rows = seq_len // GRID_W
    row_id = jnp.broadcast_to(jnp.arange(rows)[:, None], (rows, GRID_W)).reshape(-1).astype(jnp.float32)
    col_id = jnp.broadcast_to(jnp.arange(GRID_W)[None, :], (rows, GRID_W)).reshape(-1).astype(jnp.float32)
    axis_dim = HEAD_DIM // 2
    inv_freq = jnp.power(jnp.float32(ROPE_THETA), -jnp.arange(0, axis_dim, 2, dtype=jnp.float32) / axis_dim)
    ang_r = row_id[:, None] * inv_freq[None, :]
    ang_c = col_id[:, None] * inv_freq[None, :]
    ang = jnp.concatenate([ang_r, ang_r, ang_c, ang_c], axis=-1)
    return jnp.cos(ang), jnp.sin(ang)

def rotate_half(a):
    a1, a2 = jnp.split(a, 2, axis=-1)
    return jnp.concatenate([-a2, a1], axis=-1)

def apply_axial_rope(x, cos, sin):
    xr, xc = jnp.split(x, 2, axis=-1)
    rot = jnp.concatenate([rotate_half(xr), rotate_half(xc)], axis=-1)
    return x * cos + rot * sin

def block_attention(q, k, v):
    B, S = q.shape[0], q.shape[1]
    groups = N_Q_HEADS // N_KV_HEADS
    nb = S // Q_BLOCK
    qb = q.reshape(B, nb, Q_BLOCK, N_KV_HEADS, groups, HEAD_DIM).transpose(1, 0, 2, 3, 4, 5)
    scale = jnp.float32(HEAD_DIM ** -0.5)

    def one_block(qi):
        s = jnp.einsum('bqkgd,bskd->bkgqs', qi, k, preferred_element_type=jnp.float32) * scale
        p = jax.nn.softmax(s, axis=-1)
        return jnp.einsum('bkgqs,bskd->bqkgd', p.astype(v.dtype), v)

    ob = lax.map(one_block, qb)
    return ob.transpose(1, 0, 2, 3, 4, 5).reshape(B, S, ATTN_WIDTH)

def chunked_token_mlp(z, g_v, w_s, b_s):
    B, S = z.shape[0], z.shape[1]
    nc = S // CHUNK
    z = jax.nn.gelu(z)
    u, v = jnp.split(z, 2, axis=-1)
    v = rmsnorm(v.reshape(B, S, N_TOK_HEADS, HEAD_DIM), g_v)
    v = v.reshape(B, nc, CHUNK, N_TOK_HEADS, HEAD_DIM)
    mixed = jnp.einsum('hpq,bcqhd->bcphd', w_s, v) + b_s.T[None, None, :, :, None]
    out = u.reshape(B, nc, CHUNK, N_TOK_HEADS, HEAD_DIM) * mixed
    return out.reshape(B, S, TOK_WIDTH)

def conv_glu_ffn(h, w_up, w_conv, b_conv, w_down):
    z = h @ w_up
    zp = jnp.pad(z, ((0, 0), (1, 1), (0, 0)))
    z = zp[:, :-2] * w_conv[0] + zp[:, 1:-1] * w_conv[1] + zp[:, 2:] * w_conv[2] + b_conv
    a, b = jnp.split(z, 2, axis=-1)
    return (jax.nn.silu(a) * b) @ w_down

def first_inputs(seed: int = 0) -> dict:
    key = jax.random.key(seed)
    ks = jax.random.split(key, 24)
    f32 = jnp.float32
    L, D = DEPTH, D_MODEL

    def nrm(k, shape, scale):
        return jax.random.normal(k, shape, f32) * scale

    def gain(k, shape):
        return 1.0 + 0.05 * jax.random.normal(k, shape, f32)

    return {
        "x": nrm(ks[0], (BATCH, SEQ, D), 1.0),
        "c": nrm(ks[1], (BATCH, D), 1.0),
        "w_ada": nrm(ks[2], (L, D, N_MOD * D), 0.5 * D ** -0.5),
        "b_ada": nrm(ks[3], (L, N_MOD * D), 0.01),
        "g_norm1": gain(ks[4], (L, D)),
        "w_in": nrm(ks[5], (L, D, N_IN), D ** -0.5),
        "g_q": gain(ks[6], (L, HEAD_DIM)),
        "g_k": gain(ks[7], (L, HEAD_DIM)),
        "g_tok_v": gain(ks[8], (L, HEAD_DIM)),
        "w_s": nrm(ks[9], (L, N_TOK_HEADS, CHUNK, CHUNK), CHUNK ** -0.5),
        "b_s": 1.0 + nrm(ks[10], (L, N_TOK_HEADS, CHUNK), 0.01),
        "g_attn_out": gain(ks[11], (L, ATTN_WIDTH)),
        "g_tok_out": gain(ks[12], (L, TOK_WIDTH)),
        "w_out": nrm(ks[13], (L, MIX_WIDTH, D), MIX_WIDTH ** -0.5),
        "g_norm2": gain(ks[14], (L, D)),
        "w_up": nrm(ks[15], (L, D, 2 * D_FF), D ** -0.5),
        "w_conv": nrm(ks[16], (L, CONV_W, 2 * D_FF), CONV_W ** -0.5),
        "b_conv": nrm(ks[17], (L, 2 * D_FF), 0.01),
        "w_down": nrm(ks[18], (L, D_FF, D), D_FF ** -0.5),
        "g_final": gain(ks[19], (D,)),
    }

def first_block(x, c, w_ada, b_ada, g_norm1, w_in, g_q, g_k, g_tok_v, w_s, b_s,
              g_attn_out, g_tok_out, w_out, g_norm2, w_up, w_conv, b_conv, w_down, g_final):
    B, S, _ = x.shape
    cos, sin = axial_rope_tables(S)
    cos = cos.astype(x.dtype)[None, :, None, :]
    sin = sin.astype(x.dtype)[None, :, None, :]
    mod_all = jnp.einsum('bd,ldm->lbm', jax.nn.silu(c), w_ada) + b_ada[:, None, :]

    for l in range(DEPTH):
        sh1, sc1, gt1, sh2, sc2, gt2 = jnp.split(mod_all[l][:, None, :], N_MOD, axis=-1)

        h = rmsnorm(x, g_norm1[l]) * (1.0 + sc1) + sh1
        proj = h @ w_in[l]
        q, k, v, z = jnp.split(
            proj, [ATTN_WIDTH, ATTN_WIDTH + KV_WIDTH, ATTN_WIDTH + 2 * KV_WIDTH], axis=-1)
        q = rmsnorm(q.reshape(B, S, N_Q_HEADS, HEAD_DIM), g_q[l])
        k = rmsnorm(k.reshape(B, S, N_KV_HEADS, HEAD_DIM), g_k[l])
        q = apply_axial_rope(q, cos, sin)
        k = apply_axial_rope(k, cos, sin)
        v = v.reshape(B, S, N_KV_HEADS, HEAD_DIM)
        attn = block_attention(q, k, v)
        tok = chunked_token_mlp(z, g_tok_v[l], w_s[l], b_s[l])
        mixed = jnp.concatenate(
            [rmsnorm(attn, g_attn_out[l]), rmsnorm(tok, g_tok_out[l])], axis=-1)
        x = x + gt1 * (mixed @ w_out[l])

        h = rmsnorm(x, g_norm2[l]) * (1.0 + sc2) + sh2
        x = x + gt2 * conv_glu_ffn(h, w_up[l], w_conv[l], b_conv[l], w_down[l])

    return rmsnorm(x, g_final)


SSM_D_INNER = D_MODEL
SSM_HEAD_DIM = 64
SSM_HEADS = SSM_D_INNER // SSM_HEAD_DIM
SSM_GROUPS = 4
SSM_STATE = 128
SSM_CONV = 4
SSM_CHUNK = 128
SSM_CONV_DIM = SSM_D_INNER + 2 * SSM_GROUPS * SSM_STATE
ATT_D = D_MODEL
ATT_HEAD_DIM = 64
ATT_HEADS = ATT_D // ATT_HEAD_DIM
ATT_BLOCK = 128
RMS_EPS = 1e-6
IN_SPLITS = (SSM_D_INNER, SSM_CONV_DIM, SSM_HEADS, ATT_D, ATT_D, ATT_D, ATT_HEADS, ATT_D, D_MODEL, D_MODEL)
IN_COLS = SSM_D_INNER + SSM_CONV_DIM + SSM_HEADS + 4 * ATT_D + ATT_HEADS + 2 * D_MODEL


def _offsets(sizes):
    out, acc = [], 0
    for s in sizes[:-1]:
        acc += s
        out.append(acc)
    return out

def _rmsnorm(x, g):
    xf = x.astype(jnp.float32)
    y = xf * lax.rsqrt(jnp.mean(xf * xf, axis=-1, keepdims=True) + RMS_EPS) * g.astype(jnp.float32)
    return y.astype(x.dtype)

def _causal_dwconv(u, w, b):
    y = lax.conv_general_dilated(u, w[:, None, :].astype(u.dtype), window_strides=(1,),
                                 padding=((SSM_CONV - 1, 0),),
                                 dimension_numbers=('NWC', 'WIO', 'NWC'),
                                 feature_group_count=u.shape[-1])
    return y + b.astype(u.dtype)

def _ssd_chunked(xs, dt, a, b_mat, c_mat, d_skip):
    bsz, seqlen, n_heads, p = xs.shape
    g, n = b_mat.shape[2], b_mat.shape[3]
    r = n_heads // g
    nc = seqlen // SSM_CHUNK
    q = SSM_CHUNK
    xdt = (xs * dt[..., None]).reshape(bsz, nc, q, g, r, p)
    bc = b_mat.reshape(bsz, nc, q, g, n)
    cc = c_mat.reshape(bsz, nc, q, g, n)
    da_cs = jnp.cumsum((dt * a).reshape(bsz, nc, q, g, r), axis=2)
    causal = jnp.tril(jnp.ones((q, q), dtype=bool))
    seg = da_cs[:, :, :, None] - da_cs[:, :, None, :]
    decay = jnp.exp(jnp.where(causal[None, None, :, :, None, None], seg, -jnp.inf))
    cb = jnp.einsum('bclgn,bcsgn->bclsg', cc, bc)
    y_diag = jnp.einsum('bclsgr,bcsgrp->bclgrp', cb[..., None] * decay, xdt)
    to_end = jnp.exp(da_cs[:, :, -1:] - da_cs)
    states = jnp.einsum('bcsgn,bcsgrp->bcgrpn', bc, xdt * to_end[..., None])
    chunk_decay = jnp.exp(da_cs[:, :, -1])

    def step(carry, inp):
        st, dec = inp
        return carry * dec[..., None, None] + st, carry

    init = jnp.zeros((bsz, g, r, p, n), states.dtype)
    _, prev = lax.scan(step, init, (jnp.moveaxis(states, 1, 0), jnp.moveaxis(chunk_decay, 1, 0)))
    prev = jnp.moveaxis(prev, 0, 1)
    y_off = jnp.einsum('bclgn,bcgrpn->bclgrp', cc, prev) * jnp.exp(da_cs)[..., None]
    y = (y_diag + y_off).reshape(bsz, seqlen, n_heads, p)
    return y + xs * d_skip[:, None]

def _forgetting_attention(q, k, v, log_f):
    seqlen = q.shape[2]
    scale = ATT_HEAD_DIM ** -0.5
    fcum = jnp.cumsum(log_f, axis=-1)
    outs = []
    for blk in range(seqlen // ATT_BLOCK):
        q0, q1 = blk * ATT_BLOCK, (blk + 1) * ATT_BLOCK
        s = jnp.einsum('bhqd,bhkd->bhqk', q[:, :, q0:q1], k[:, :, :q1]).astype(jnp.float32) * scale
        s = s + fcum[:, :, q0:q1, None] - fcum[:, :, None, :q1]
        qpos = q0 + jnp.arange(ATT_BLOCK)
        kpos = jnp.arange(q1)
        s = jnp.where(kpos[None, :] <= qpos[:, None], s, -jnp.inf)
        prob = jax.nn.softmax(s, axis=-1)
        outs.append(jnp.einsum('bhqk,bhkd->bhqd', prob.astype(v.dtype), v[:, :, :q1]))
    return jnp.concatenate(outs, axis=2)

def _hybrid_layer(x, pre_g, w_in, conv_w, conv_b, dt_bias, a_log, d_skip, ssm_norm_g,
                  fgate_b, w_branch_ssm, w_branch_att, w_out, post_g):
    bsz, seqlen, _ = x.shape
    f32 = jnp.float32
    h = _rmsnorm(x, pre_g)
    proj = jnp.einsum('bld,de->ble', h, w_in)
    z_ssm, xbc, dt_raw, q, k, v, f_raw, z_att, g_ssm, g_att = jnp.split(proj, _offsets(IN_SPLITS), axis=-1)

    xbc = jax.nn.silu(_causal_dwconv(xbc, conv_w, conv_b))
    gn = SSM_GROUPS * SSM_STATE
    xs, b_ssm, c_ssm = jnp.split(xbc, [SSM_D_INNER, SSM_D_INNER + gn], axis=-1)
    dt = jax.nn.softplus(dt_raw.astype(f32) + dt_bias.astype(f32))
    a = -jnp.exp(a_log.astype(f32))
    y = _ssd_chunked(xs.astype(f32).reshape(bsz, seqlen, SSM_HEADS, SSM_HEAD_DIM), dt, a,
                     b_ssm.astype(f32).reshape(bsz, seqlen, SSM_GROUPS, SSM_STATE),
                     c_ssm.astype(f32).reshape(bsz, seqlen, SSM_GROUPS, SSM_STATE),
                     d_skip.astype(f32))
    yg = (y.reshape(bsz, seqlen, SSM_D_INNER) * jax.nn.silu(z_ssm.astype(f32)))
    yg = yg.reshape(bsz, seqlen, SSM_GROUPS, SSM_D_INNER // SSM_GROUPS)
    yg = yg * lax.rsqrt(jnp.mean(yg * yg, axis=-1, keepdims=True) + RMS_EPS)
    y_ssm = (yg.reshape(bsz, seqlen, SSM_D_INNER) * ssm_norm_g.astype(f32)).astype(x.dtype)

    def heads(t):
        return t.reshape(bsz, seqlen, ATT_HEADS, ATT_HEAD_DIM).transpose(0, 2, 1, 3)
    log_f = jax.nn.log_sigmoid(f_raw.astype(f32) + fgate_b.astype(f32)).transpose(0, 2, 1)
    o = _forgetting_attention(heads(q), heads(k), heads(v), log_f)
    o = o.transpose(0, 2, 1, 3).reshape(bsz, seqlen, ATT_D)
    y_att = (o.astype(f32) * jax.nn.silu(z_att.astype(f32))).astype(x.dtype)

    p_ssm = jnp.einsum('ble,ed->bld', y_ssm, w_branch_ssm)
    p_att = jnp.einsum('ble,ed->bld', y_att, w_branch_att)
    merged = jax.nn.sigmoid(g_ssm) * p_ssm + jax.nn.sigmoid(g_att) * p_att
    out = jnp.einsum('bld,de->ble', merged, w_out)
    return x + _rmsnorm(out, post_g)

def second_inputs(seed: int = 0) -> dict:
    key = jax.random.key(seed)
    ks = jax.random.split(key, 16)
    f32 = jnp.float32
    nl = DEPTH
    nrm = jax.random.normal
    x = nrm(ks[0], (BATCH, SEQ, D_MODEL), f32)
    pre_norm_g = 1.0 + 0.05 * nrm(ks[1], (nl, D_MODEL), f32)
    w_in = nrm(ks[2], (nl, D_MODEL, IN_COLS), f32) * D_MODEL ** -0.5
    conv_w = nrm(ks[3], (nl, SSM_CONV, SSM_CONV_DIM), f32) * SSM_CONV ** -0.5
    conv_b = 0.02 * nrm(ks[4], (nl, SSM_CONV_DIM), f32)
    dt0 = jnp.exp(jax.random.uniform(ks[5], (nl, SSM_HEADS), f32, minval=math.log(1e-3), maxval=math.log(1e-1)))
    dt_bias = dt0 + jnp.log(-jnp.expm1(-dt0))
    a_log = jnp.log(jax.random.uniform(ks[6], (nl, SSM_HEADS), f32, minval=1.0, maxval=16.0))
    d_skip = 1.0 + 0.1 * nrm(ks[7], (nl, SSM_HEADS), f32)
    ssm_norm_g = 1.0 + 0.05 * nrm(ks[8], (nl, SSM_D_INNER), f32)
    fgate_b = jax.random.uniform(ks[9], (nl, ATT_HEADS), f32, minval=1.0, maxval=4.0)
    w_branch_ssm = nrm(ks[10], (nl, SSM_D_INNER, D_MODEL), f32) * SSM_D_INNER ** -0.5
    w_branch_att = nrm(ks[11], (nl, ATT_D, D_MODEL), f32) * ATT_D ** -0.5
    w_out = nrm(ks[12], (nl, D_MODEL, D_MODEL), f32) * D_MODEL ** -0.5
    post_norm_g = 1.0 + 0.05 * nrm(ks[13], (nl, D_MODEL), f32)
    return {'x': x, 'pre_norm_g': pre_norm_g, 'w_in': w_in, 'conv_w': conv_w, 'conv_b': conv_b,
            'dt_bias': dt_bias, 'a_log': a_log, 'd_skip': d_skip, 'ssm_norm_g': ssm_norm_g,
            'fgate_b': fgate_b, 'w_branch_ssm': w_branch_ssm, 'w_branch_att': w_branch_att,
            'w_out': w_out, 'post_norm_g': post_norm_g}

def second_block(x, pre_norm_g, w_in, conv_w, conv_b, dt_bias, a_log, d_skip, ssm_norm_g,
              fgate_b, w_branch_ssm, w_branch_att, w_out, post_norm_g):
    for i in range(DEPTH):
        x = _hybrid_layer(x, pre_norm_g[i], w_in[i], conv_w[i], conv_b[i], dt_bias[i], a_log[i],
                          d_skip[i], ssm_norm_g[i], fgate_b[i], w_branch_ssm[i], w_branch_att[i],
                          w_out[i], post_norm_g[i])
    return x


def setup_inputs(seed=0):
    out = dict(first_inputs(seed))
    for name, value in second_inputs(seed + 1).items():
        if name != "x":
            out[name + "_2"] = value
    return out


def reference(
    x, c, w_ada, b_ada, g_norm1, w_in, g_q, g_k, g_tok_v, w_s, b_s, g_attn_out, g_tok_out,
    w_out, g_norm2, w_up, w_conv, b_conv, w_down, g_final, pre_norm_g_2, w_in_2, conv_w_2,
    conv_b_2, dt_bias_2, a_log_2, d_skip_2, ssm_norm_g_2, fgate_b_2, w_branch_ssm_2,
    w_branch_att_2, w_out_2, post_norm_g_2,
):
    x = first_block(
        x, c, w_ada, b_ada, g_norm1, w_in, g_q, g_k, g_tok_v, w_s, b_s, g_attn_out, g_tok_out,
        w_out, g_norm2, w_up, w_conv, b_conv, w_down, g_final,
    )
    return second_block(
        x, pre_norm_g_2, w_in_2, conv_w_2, conv_b_2, dt_bias_2, a_log_2, d_skip_2, ssm_norm_g_2,
        fgate_b_2, w_branch_ssm_2, w_branch_att_2, w_out_2, post_norm_g_2,
    )


_drawn_inputs = setup_inputs


def setup_inputs(seed=0):
    import zlib

    import numpy as np

    out = dict(_drawn_inputs(seed))
    spreads = {}
    factors = {'b_ada': 2.739,
     'g_norm1': 3.273,
     'g_q': 8.0,
     'g_k': 8.0,
     'g_tok_v': 6.277,
     'b_s': 8.0,
     'g_attn_out': 3.711,
     'g_tok_out': 4.104,
     'g_norm2': 3.174,
     'b_conv': 8.0,
     'conv_b_2': 2.815}
    for name, (base, spread) in spreads.items():
        noise = np.random.default_rng([zlib.crc32(name.encode()), seed]).standard_normal(out[name].shape)
        drawn = base * np.exp(spread * noise) if base else spread * noise
        out[name] = __import__('jax').numpy.asarray(drawn.astype(out[name].dtype))
    for name, factor in factors.items():
        out[name] = (out[name] * factor).astype(out[name].dtype)
    return out
```

```python
from contextlib import ExitStack

import numpy as np

import concourse.bass as bass
from concourse import mybir

F32 = mybir.dt.float32
F32R = mybir.dt.float32r
ACT = mybir.ActivationFunctionType
ALU = mybir.AluOpType
AX = mybir.AxisListType.X

T = 1024
KT = 8
NFF = 22
EPS = 1e-6
NEG = -1.0e30

PAR = [("c", 8), ("b_ada", 48), ("g1", 8), ("g2", 8), ("gf", 8), ("gpre", 8), ("gpost", 8),
       ("gq", 1), ("gk", 1), ("gv", 1), ("gao", 4), ("gto", 4), ("wc", 132), ("bc", 44),
       ("wc2", 64), ("bc2", 16), ("rowb", 1), ("rowa", 1), ("dskip", 8), ("gssm", 8)]
POFF = {}
NPAR = 0
for _n, _w in PAR:
    POFF[_n] = NPAR
    NPAR += _w

FG = [4, 4, 4, 4, 4, 2]


def plan():
    s = [("a", m, k) for m in (1, 0) for k in range(KT)]
    later = [("a", m, k) for m in (2, 4, 3, 5) for k in range(KT)]
    first = [("w", "in", n) for n in range(14)]
    for n, b in enumerate(first):
        s.append(b)
        if n >= 1:
            s += [later.pop(0) for _ in range(min(3, len(later)))]
    s += later
    s += [("w", "out", n) for n in range(8)]
    f0 = 0
    s += [("w", "up", 0), ("w", "up", NFF)]
    for g, n in enumerate(FG):
        for f in range(f0 + 1, min(f0 + n + 1, NFF)):
            s += [("w", "up", f), ("w", "up", NFF + f)]
        s += [("w", "down%d" % g, b) for b in range(n)]
        f0 += n
    s.append(("w", "dtf", 0))
    for g in range(4):
        s += [("w", "xs", 2 * g), ("w", "xs", 2 * g + 1), ("w", "B", g), ("w", "C", g)]
        s += [("w", "z", 2 * g), ("w", "z", 2 * g + 1), ("w", "gs", 2 * g), ("w", "gs", 2 * g + 1)]
    s.append(("w", "k", 0))
    for p in range(8):
        s += [("w", "q", p), ("w", "v", p), ("w", "za", p), ("w", "ga", p)]
        if p < 7:
            s.append(("w", "k", p + 1))
    for name in ("bs", "ba", "out2"):
        s += [("w", name, n) for n in range(8)]
    return s


class Queues:

    ENG = ("pe", "act", "dve", "pool", "sp")

    def __init__(self, nc, ctx):
        self.q = {e: [] for e in self.ENG}
        self.sem = {e: ctx.enter_context(nc.semaphore("done_" + e)) for e in self.ENG if e != "sp"}
        self.n = {e: 0 for e in self.sem}
        self.seen = {e: {} for e in self.ENG}
        self.ndma = 40
        self.dn = [0] * self.ndma
        self.di = 0
        for i in range(self.ndma):
            self.sem["d%d" % i] = ctx.enter_context(nc.semaphore("dma%d" % i))

    def wait(self, eng, toks):
        for s, v in sorted(toks, key=lambda t: -t[1]):
            if self.seen[eng].get(s, 0) < v:
                self.seen[eng][s] = v
                sem = self.sem[s]
                self.q[eng].append(lambda e, sem=sem, v=v: e.wait_ge(sem, v))

    def op(self, eng, fn, toks=(), inc=True):
        self.wait(eng, toks)
        if not inc:
            self.q[eng].append(fn)
            return None
        self.n[eng] += 1
        sem = self.sem[eng]
        self.q[eng].append(lambda e: fn(e).then_inc(sem, 1))
        return (eng, self.n[eng])

    def pe(self, fn, toks=(), inc=True):
        return self.op("pe", fn, toks, inc)

    def act(self, fn, toks=()):
        return self.op("act", fn, toks)

    def dve(self, fn, toks=()):
        return self.op("dve", fn, toks)

    def pool(self, fn, toks=()):
        return self.op("pool", fn, toks)

    def dma(self, out, in_, toks=()):
        i = self.di % self.ndma
        self.di += 1
        if self.dn[i]:
            self.wait("sp", [("d%d" % i, self.dn[i])])
        self.wait("sp", toks)
        self.dn[i] += 16
        sem = self.sem["d%d" % i]
        self.q["sp"].append(lambda e: e.dma_start(out, in_).then_inc(sem, 16))
        return ("d%d" % i, self.dn[i])

    def sofar(self):
        return [(e, n) for e, n in self.n.items() if n]


def v3(ap, n=128):
    return ap.rearrange("p (c n) -> p c n", n=n)


class Kernel:

    def __init__(self, nc, ctx, d):
        self.nc, self.d = nc, d
        self.k = Queues(nc, ctx)
        base = (nc.sbuf_base + 31) // 32 * 32
        kb = 1024

        def at(name, cols, dt, off):
            return nc.alloc_sbuf_tensor_at(name, [128, cols], dt, offset=base + off)

        self.hl = at("hl", 3 * 2048, F32R, 0)
        self.raw = at("raw", 3 * 1024, F32, 24 * kb)
        self.ht = at("ht", 16 * 1024, F32R, 36 * kb)
        self.htf = at("htf", 16 * 1024, F32, 36 * kb)
        self.wr = at("wr", 24 * 1024, F32R, 100 * kb)
        self.wf = at("wf", 24 * 1024, F32, 100 * kb)
        m = [196 * kb]

        def small(name, cols, dt=F32):
            t = at(name, cols, dt, m[0])
            m[0] += (cols * 4 + 31) // 32 * 32
            assert base + m[0] <= nc.sbuf_usable_end, m[0]
            return t

        self.cst = small("cst", 7 * 128)
        self.par = small("par", NPAR)
        self.bsb = small("bsb", 512)
        self.col = small("col", 128)
        self.st = small("st", 64)
        self.idr = small("idr", 128, F32R)
        self.maskr = small("maskr", 128, F32R)
        self.rcol = small("rcol", 4)
        self.end = small("end", 128)
        self.dec = small("dec", 128)
        self.sm = small("sm", 128)
        self.sm_i = 0
        self.sm_read = [[] for _ in range(8)]
        self.c_id, self.c_one, self.c_bd, self.c_perm, self.c_last, self.c_mask, self.mask01 = (
            self.cst[:, 128 * i:128 * i + 128] for i in range(7))
        self.ps = [nc.alloc_psum_tensor("ps%d" % i, [128, 1024], F32) for i in range(4)]
        self.made = [[] for _ in range(8)]
        self.taken = [[] for _ in range(8)]
        self.hready = [[[] for _ in range(8)] for _ in range(2)]
        self.hused = []
        self.plan = plan()
        self.wlist = [i for i, s in enumerate(self.plan) if s[0] == "w"]
        self.nd = self.np = self.nw = self.wi = 0
        self.cur = None
        self.raw_loaded = [[] for _ in range(3)]
        self.raw_read = [[] for _ in range(3)]
        self.hl_parted = [[] for _ in range(3)]
        self.hl_used = [[] for _ in range(3)]
        self.slot_of = {}
        self.fillers = []
        self.stored = {}
        self.mods = {}

    def w(self, i, n=1):
        return self.wf[:, i * 1024:(i + n) * 1024]

    def wrr(self, i, n=1):
        return self.wr[:, i * 1024:(i + n) * 1024]

    def p(self, name, j=0, n=1):
        o = POFF[name] + j
        return self.par[:, o:o + n]

    def hth(self, k):
        return self.ht[:, k * 1024:(k + 1) * 1024]

    def htl(self, k):
        return self.ht[:, (8 + k) * 1024:(9 + k) * 1024]

    def htlf(self, k):
        return self.htf[:, (8 + k) * 1024:(9 + k) * 1024]

    def mod(self, m, j):
        return self.col[:, 8 + 8 * m + j:9 + 8 * m + j]

    def full(self, pair):
        return self.made[2 * pair] + self.made[2 * pair + 1]

    def took(self, pair, *toks):
        self.taken[2 * pair] = list(toks)
        self.taken[2 * pair + 1] = list(toks)

    def load_to(self, j):
        while self.nd <= min(j, len(self.plan) - 1):
            i = self.nd
            s = i % 3
            if i >= 16:
                if i - 3 >= self.np:
                    return
                self.raw_loaded[s] = [self.k.dma(self.raw[:, s * 1024:(s + 1) * 1024],
                                                 self.d["wst"][i], self.raw_read[s])]
            self.nd += 1

    def process(self):
        k, i = self.k, self.np
        self.load_to(i)
        kind, name, n = self.plan[i]
        s = i % 3
        src = self.raw[:, s * 1024:(s + 1) * 1024]
        loaded = self.raw_loaded[s]
        if kind == "w":
            u = self.nw % 3
            self.nw += 1
            hi = self.hl[:, u * 2048:u * 2048 + 1024]
            lo = self.hl[:, u * 2048 + 1024:u * 2048 + 2048]
            t1 = k.act(lambda e: e.activation(hi, src, ACT.Copy), loaded + self.hl_used[u])
            t2 = k.pool(lambda e: e.tensor_tensor(lo, src, hi.bitcast(F32), ALU.subtract),
                        loaded + [t1] + self.hl_used[u])
            self.raw_read[s] = [t1, t2]
            self.hl_parted[u] = [t1, t2]
            self.slot_of[i] = u
        else:
            if i < 16:
                src, loaded = self.htf[:, i * 1024:(i + 1) * 1024], self.early[i]
            a = self.w(23)
            cc = self.csilu[:, n:n + 1]
            if n == 0:
                t = k.dve(lambda e: e.tensor_scalar(a, src, cc, None, ALU.mult),
                          loaded + self.silu_c + self.mod_used)
            else:
                t = k.dve(lambda e: e.scalar_tensor_tensor(
                    out=a, in0=src, scalar=cc, in1=a, op0=ALU.mult, op1=ALU.add),
                    loaded + [self.mod_added])
            self.mod_added = t
            if i >= 16:
                self.raw_read[s] = [t]
            if n == KT - 1:
                self.mod_column(name)
        self.np += 1
        self.load_to(self.np + 2)

    def ahead(self, i):
        later = [j for j in self.wlist if j > i][:2]
        last = later[-1] if later else len(self.plan) - 1
        while self.np <= last:
            self.process()

    def mod_column(self, m):
        k, a = self.k, self.w(23)
        ps = self.ps[3][:, 512:520]
        for j in range(8):
            t = k.pe(lambda e, j=j: e.matmul(ps[:, j:j + 1], a[:, j * 128:(j + 1) * 128],
                                             self.c_one[:, 0:1], start=True, stop=True),
                     [self.mod_added] + self.taken[7] + self.c, inc=(j == 7))
        self.mod_used = [t]
        o = self.col[:, 8 + 8 * m:16 + 8 * m]
        t2 = k.dve(lambda e: e.tensor_tensor(o, ps, self.p("b_ada", 8 * m, 8), ALU.add),
                   [t] + self.c)
        self.taken[7] = [t2]
        self.mods[m] = [t2]

    def dense(self, key, pair, kt=KT, n0=0, nk=None, x=None, halves=(0, 1), bank=None):
        k = self.k
        if self.cur != key:
            i = self.wlist[self.wi]
            assert self.plan[i][1:] == key, (self.plan[i], key)
            self.ahead(i)
            self.wi += 1
            self.cur, self.cur_i = key, i
        s = self.slot_of[self.cur_i]
        nk = nk or kt
        ht = x is None
        if ht:
            x = [(self.hth(j), self.htl(j), (self.hready[0][j], self.hready[1][j]))
                 for j in range(8)]
        for h in halves:
            b = 2 * pair + (h if bank is None else bank)
            out = self.ps[pair][:, (b % 2) * 512:(b % 2 + 1) * 512]
            for j in range(kt):
                w0 = s * 2048 + n0 + j * (1024 // nk)
                wh = self.hl[:, w0:w0 + 128]
                wl = self.hl[:, w0 + 1024:w0 + 1152]
                xh, xl, xr = x[j]
                for q, (a, m) in enumerate(((wh, xh), (wh, xl), (wl, xh))):
                    last = j == kt - 1 and q == 2
                    t = k.pe(lambda e, a=a, m=m, q=q, j=j, last=last, out=out, h=h: e.matmul(
                        out, a, m[:, h * 512:(h + 1) * 512], start=(j == 0 and q == 0), stop=last),
                        self.taken[b] + self.hl_parted[s] + xr[h] if q == 0 else (), inc=last)
                if j < kt - 1:
                    yield
            self.made[b] = [t]
            self.hl_used[s] = [t]
            self.lastx = [t]
            if ht:
                self.hused = [t]
            yield

    def run(self, gen):
        for _ in gen:
            pass

    def fill(self, n):
        while n > 0 and self.fillers:
            try:
                next(self.fillers[0])
                n -= 1
            except StopIteration:
                self.fillers.pop(0)

    def flush(self):
        while self.fillers:
            self.fill(1)

    def split(self, src, ready, hi, lo, free, h, eng="dve"):
        k = self.k
        c = slice(h * 512, (h + 1) * 512)
        t1 = k.act(lambda e: e.activation(hi[:, c], src[:, c], ACT.Copy), ready + free)
        t2 = k.op(eng, lambda e: e.tensor_tensor(lo[:, c], src[:, c], hi[:, c].bitcast(F32),
                                                 ALU.subtract), ready + [t1] + free)
        return [t1, t2]

    def square_add(self, x, ready, scale, first, acc_i, acc, tmp_i, tmp_free):
        k, a, t = self.k, self.w(acc_i), self.w(tmp_i)
        if first:
            t1 = k.act(lambda e: e.activation(a, x, ACT.Square, scale=scale), ready + acc)
            return [t1], [t1]
        t1 = k.act(lambda e: e.activation(t, x, ACT.Square, scale=scale), ready + tmp_free)
        t2 = k.dve(lambda e: e.tensor_tensor(a, a, t, ALU.add), acc + [t1])
        return [t2], [t1]

    def times(self, mat, y_i, ready, pair):
        k = self.k
        for h in (0, 1):
            b = 2 * pair + h
            x = self.w(y_i)[:, h * 512:(h + 1) * 512]
            t = k.pe(lambda e, x=x, h=h: e.matmul(self.ps[pair][:, h * 512:(h + 1) * 512], mat, x,
                                                  start=True, stop=True),
                     self.c + ready + self.taken[b])
            self.made[b] = [t]
        return t

    def sums(self, tiles, ready, ncol, pair):
        k = self.k
        rhs = self.c_one[:, 0:1] if ncol == 1 else self.cst[:, 256:384:64]
        b = 2 * pair
        for c in range(8):
            for n, i in enumerate(tiles):
                last = c == 7 and n == len(tiles) - 1
                t = k.pe(lambda e, c=c, n=n, i=i: e.matmul(
                    self.ps[pair][:, c * ncol:(c + 1) * ncol], self.w(i)[:, c * 128:(c + 1) * 128],
                    rhs, start=(n == 0), stop=(n == len(tiles) - 1)),
                    self.c + ready + self.taken[b], inc=last)
        self.made[b] = [t]
        return t

    def small(self):
        i = self.sm_i % 8
        self.sm_i += 1
        return self.sm[:, 16 * i:16 * i + 16], i

    def rsqrt(self, pair, ncol, scale, eps_col):
        k, b = self.k, 2 * pair
        r, i = self.small()
        r = r[:, 0:8 * ncol]
        t = k.act(lambda e: e.activation(r, self.ps[pair][:, 0:8 * ncol], ACT.Sqrt, bias=eps_col,
                                         scale=scale), self.made[b] + self.sm_read[i] + self.c)
        self.taken[b] = [t]
        t2 = k.dve(lambda e: e.reciprocal(r, r), [t])
        return r, i, t2

    def spread(self, r, i, ready, ncol, tmp_i, tmp_free, pair):
        k = self.k
        n = 128 // ncol
        tc = k.dve(lambda e: e.tensor_copy(
            self.w(tmp_i).rearrange("p (c n) -> p c n", n=n),
            r.unsqueeze(2).broadcast_to([128, 8 * ncol, n])), [ready] + tmp_free)
        self.sm_read[i] = [tc]
        for h in (0, 1):
            b = 2 * pair + h
            for c in range(4 * h, 4 * h + 4):
                t = k.pe(lambda e, c=c: e.matmul(
                    self.ps[pair][:, c * 128:(c + 1) * 128],
                    self.w(tmp_i)[:, c * 128:(c + 1) * 128], self.c_id, start=True, stop=True),
                    self.c + [tc] + self.taken[b], inc=(c % 4 == 3))
            self.made[b] = [t]
        return t

    def rnorm(self, tiles, ready, ncol, scale, eps_col, tmp_i, tmp_free, pair):
        self.sums(tiles, ready, ncol, pair)
        r, i, t = self.rsqrt(pair, ncol, scale, eps_col)
        return self.spread(r, i, t, ncol, tmp_i, tmp_free, pair)

    def keep(self, pair, r_i, free):
        t = self.k.act(lambda e: e.activation(self.w(r_i), self.ps[pair][:, :], ACT.Copy),
                       self.full(pair) + free)
        self.took(pair, t)
        return t

    def norm_split(self, j, src, ready, g, r_i, rt, tmp_i, tmp_free, free, h, affine=None,
                   eng="dve"):
        k = self.k
        c = slice(h * 512, (h + 1) * 512)
        y, r = self.w(tmp_i), self.w(r_i)
        if affine is None:
            t = k.dve(lambda e: e.scalar_tensor_tensor(
                out=y[:, c], in0=src[:, c], scalar=g, in1=r[:, c], op0=ALU.mult, op1=ALU.mult),
                ready + [rt] + tmp_free + self.c)
        else:
            a, b, at = affine
            t0 = k.dve(lambda e: e.tensor_tensor(y[:, c], src[:, c], r[:, c], ALU.mult),
                       ready + [rt] + tmp_free)
            t = k.act(lambda e: e.activation(y[:, c], y[:, c], ACT.Identity, bias=b, scale=a),
                      [t0] + at)
        parts = self.split(y, [t], self.hth(j), self.htl(j), free, h, eng)
        self.hready[h][j] = parts
        return parts

    def to_tokens(self, y_i, ready, pair):
        k, y = self.k, self.w(y_i)
        for h in (0, 1):
            b = 2 * pair + h
            for c in range(4 * h, 4 * h + 4):
                t = k.pe(lambda e, c=c: e.transpose(self.ps[pair][:, c * 128:(c + 1) * 128],
                                                    y[:, c * 128:(c + 1) * 128], self.c_id),
                         ready + self.c + self.taken[b], inc=(c % 4 == 3))
            self.made[b] = [t]
        return t

    def stack_v(self, pair, tiles, free):
        k = self.k
        ps = v3(self.ps[pair][:, :])
        ta, td = [], []
        for hh in (0, 1):
            dst = v3(self.wrr(tiles[hh]))
            s = slice(64 * hh, 64 * hh + 64)
            ta.append(k.act(lambda e, s=s, dst=dst: e.activation(dst[:, :, 0:64], ps[:, :, s],
                                                                 ACT.Copy), self.full(pair) + free))
        for hh in (0, 1):
            dst = v3(self.wrr(tiles[hh]))
            dstf = v3(self.wrr(tiles[hh]).bitcast(F32))
            s = slice(64 * hh, 64 * hh + 64)
            td.append(k.dve(lambda e, s=s, dst=dst, dstf=dstf: e.tensor_tensor(
                dst[:, :, 64:128], ps[:, :, s], dstf[:, :, 0:64], ALU.subtract),
                self.full(pair) + ta + free))
        self.took(pair, *ta, *td)
        return ta + td

    def stack(self, src, ready, hi, lo, free, scale=1.0, twice=False):
        k = self.k
        ta, td = [], []
        for hh in (0, 1):
            a = slice(64 * hh, 64 * hh + 64)
            o = slice(64 - 64 * hh, 128 - 64 * hh)
            dst = self.wrr(hi[hh])
            for r in (a, o) if twice else (a,):
                ta.append(k.act(lambda e, a=a, r=r, dst=dst: e.activation(
                    dst[r, :], src[a, :], ACT.Copy, scale=scale), ready + free))
        for hh in (0, 1):
            a = slice(64 * hh, 64 * hh + 64)
            o = slice(64 - 64 * hh, 128 - 64 * hh)
            dst, f = self.wrr(lo[hh]), self.wrr(hi[hh]).bitcast(F32)
            for r in (a, o) if twice else (o,):
                td.append(k.dve(lambda e, a=a, r=r, dst=dst, f=f: e.scalar_tensor_tensor(
                    out=dst[r, :], in0=src[a, :], scalar=scale, in1=f[a, :], op0=ALU.mult,
                    op1=ALU.subtract), ready + ta + free))
        return ta + td

    def start(self):
        k, d = self.k, self.d
        self.csilu = self.col[:, 0:8]
        self.mod_used = []
        loads = [k.dma(self.par[:, :], d["par"]), k.dma(self.cst[:, :], d["cst"])]
        self.xt, self.early = [], []
        for j in range(8):
            self.xt.append([k.dma(self.w(j), d["xT"][j * 128:(j + 1) * 128, :])])
            self.early.append([k.dma(self.htf[:, j * 1024:(j + 1) * 1024], d["wst"][j])])
        for j in range(8, 16):
            self.early.append([k.dma(self.htf[:, j * 1024:(j + 1) * 1024], d["wst"][j])])
        loads.append(k.dma(self.bsb[:, :], d["bsb"]))
        self.silu_c = [k.act(lambda e: e.activation(self.csilu, self.p("c", 0, 8), ACT.Silu),
                             loads[0:1])]
        self.eps, self.eps64, self.onev = (self.rcol[:, j:j + 1] for j in range(3))
        t1 = k.pool(lambda e: e.memset(self.eps, EPS))
        t2 = k.pool(lambda e: e.memset(self.eps64, 64.0 * EPS))
        t3 = k.pool(lambda e: e.memset(self.onev, 1.0))
        t4 = k.act(lambda e: e.activation(self.idr[:, :], self.c_id, ACT.Copy), loads)
        t5 = k.act(lambda e: e.activation(self.maskr[:, :], self.c_mask, ACT.Copy, scale=-NEG,
                                          bias=NEG), loads)
        self.c = [*loads, t1, t2, t3, t4, t5]

    def norm1(self):
        k = self.k
        acc, adds = [], {}
        for j in range(8):
            acc, _ = self.square_add(self.w(j), self.xt[j], 1.0, j == 0, 8, acc, 9 + j % 2,
                                     adds.get(j - 2, []))
            adds[j] = acc
            self.process()
        self.rnorm([8], acc, 1, 1.0 / 1024, self.eps, 11, [], 0)
        rt = self.keep(0, 12, [])
        while self.np < 16:
            self.process()
        a = self.col[:, 64:72]
        ta = k.dve(lambda e: e.scalar_tensor_tensor(
            out=a, in0=self.col[:, 16:24], scalar=1.0, in1=self.p("g1", 0, 8), op0=ALU.add,
            op1=ALU.mult), self.mods[1] + self.c)
        self.load_to(18)
        free = self.mods[0] + self.mods[1]
        tmp = {}
        n = 0
        for h in (0, 1):
            for j in range(8):
                tmp[n] = self.norm_split(j, self.w(j), self.xt[j], None, 12, rt, 13 + n % 4,
                                         tmp.get(n - 4, []), free, h,
                                         (a[:, j:j + 1], self.mod(0, j), [ta] + self.mods[0]),
                                         "pool" if j % 2 else "dve")
                n += 1
            if h == 0:
                self.ahead(self.wlist[0] - 1)

    def project1(self):
        k, d = self.k, self.d
        COS, SIN = 14, 15
        old = k.sofar()
        tab = [k.dma(self.w(COS), d["rope"][0], old), k.dma(self.w(SIN), d["rope"][1], old)]
        yfree, sfree = {0: old, 1: old}, {0: old, 1: old}
        self.f22 = old
        self.rot_used, self.ready = [], {}

        def qk_tail(n, pair):
            g = self.p("gq") if n < 4 else self.p("gk")
            u = n % 2
            y_i, s_i = 18 + 2 * u, 19 + 2 * u
            y, s = self.w(y_i), self.w(s_i)
            ps = self.ps[pair]
            t1 = k.act(lambda e: e.activation(s, ps[:, :], ACT.Square), self.full(pair) + sfree[u])
            t2 = k.act(lambda e: e.activation(y, ps[:, :], ACT.Copy, scale=g),
                       self.full(pair) + yfree[u] + self.c)
            self.took(pair, t1, t2)
            yield
            tsum = self.sums([s_i], [t1], 2, 2)
            trot = self.times(self.c_perm, y_i, [t2], 3)
            r, i, tr = self.rsqrt(2, 2, 1.0 if n < 4 else 1.0 / 64,
                                  self.eps64 if n < 4 else self.eps)
            t4 = k.pool(lambda e: e.tensor_tensor(y, y, self.w(COS), ALU.mult), [t2, trot] + tab)
            yield
            tsp = self.spread(r, i, tr, 2, 22, self.f22, 2)
            self.f22 = [tsp]
            t3 = k.dve(lambda e: e.tensor_tensor(s, self.ps[3][:, :], self.w(SIN), ALU.mult),
                       self.full(3) + tab + [tsum])
            self.took(3, t3)
            t5 = k.dve(lambda e: e.tensor_tensor(y, y, s, ALU.add), [t3, t4])
            t6 = k.dve(lambda e: e.tensor_tensor(y, y, self.ps[2][:, :], ALU.mult),
                       [t5] + self.full(2))
            self.took(2, t6)
            self.rot_used = [t3, t4]
            if n < 4:
                tiles = (2 * n, 2 * n + 1)
                ts = self.stack(y, [t6], tiles, tiles, old)
                self.ready["q", 2 * n] = self.ready["q", 2 * n + 1] = ts
            else:
                ts = self.stack(y, [t6], (8, 10), (9, 11), old, 1.0, True)
                self.ready["k"] = ts
            yfree[u] = ts
            sfree[u] = [t5]
            yield

        def v_tail(n, pair):
            u = n % 2
            y_i = 18 + 2 * u
            t = k.act(lambda e: e.activation(self.w(y_i), self.ps[pair][:, :], ACT.Copy),
                      self.full(pair) + yfree[u])
            self.took(pair, t)
            yield
            tt = self.to_tokens(y_i, [t], 2)
            yfree[u] = [tt]
            yield
            self.ready["v"] = self.stack_v(2, (12, 13), old)
            yield

        def u_tail(n, pair):
            t = k.act(lambda e: e.activation(self.w(14 + n), self.ps[pair][:, :],
                                             ACT.Gelu_apprx_tanh),
                      self.full(pair) + self.rot_used + old)
            self.took(pair, t)
            self.ready["u", n] = t
            yield

        def z_tail(n, pair):
            u = n % 2
            y_i, s_i = 18 + 2 * u, 19 + 2 * u
            y, s, ws = self.w(y_i), self.w(s_i), self.w(22)
            if n == 0:
                self.ws_loaded = k.dma(ws, d["wsT"], self.f22)
            t = k.act(lambda e: e.activation(y, self.ps[pair][:, :], ACT.Gelu_apprx_tanh),
                      self.full(pair) + yfree[u])
            self.took(pair, t)
            t1 = k.act(lambda e: e.activation(s, y, ACT.Square), [t] + sfree[u])
            yield
            tsum = self.sums([s_i], [t1], 2, 2)
            r, i, tr = self.rsqrt(2, 2, 1.0 / 64, self.eps)
            yield
            tsp = self.spread(r, i, tr, 2, s_i, [tsum], 2)
            t2 = k.dve(lambda e: e.scalar_tensor_tensor(
                out=y, in0=y, scalar=self.p("gv"), in1=self.ps[2][:, :], op0=ALU.mult,
                op1=ALU.mult), [t, t1] + self.full(2) + self.c)
            self.took(2, t2)
            yield
            tt = self.to_tokens(y_i, [t2], 3)
            t3 = k.act(lambda e: e.activation(y, self.ps[3][:, :], ACT.Copy),
                       self.full(3) + [tt])
            self.took(3, t3)
            yield
            for c in range(8):
                b = 4 + c // 4
                for hh in (0, 1):
                    hd = 2 * n + hh
                    a = slice(64 * hh, 64 * hh + 64)
                    tm = k.pe(lambda e, c=c, a=a, hd=hd: e.matmul(
                        self.ps[2][a, c * 128:(c + 1) * 128],
                        y[:, c * 128 + a.start:c * 128 + a.stop],
                        ws[:, hd * 128:(hd + 1) * 128], start=True, stop=True),
                        [t3, self.ws_loaded] + self.taken[b], inc=(c % 4 == 3 and hh == 1))
                if c % 4 == 3:
                    self.made[b] = [tm]
            yfree[u] = [tm]
            yield
            bs = self.bsb[:, n * 128:(n + 1) * 128].unsqueeze(1).broadcast_to([128, 8, 128])
            t5 = k.dve(lambda e: e.tensor_tensor(v3(s), v3(self.ps[2][:, :]), bs, ALU.add),
                       self.full(2) + [tsp] + self.c)
            self.took(2, t5)
            x = self.w(14 + n)
            t6 = k.dve(lambda e: e.tensor_tensor(x, x, s, ALU.mult), [t5, self.ready["u", n]])
            sfree[u] = [t6]
            self.ready["tok", n] = t6
            yield

        def tail_of(n, pair):
            if n < 5:
                return qk_tail(n, pair)
            if n == 5:
                return v_tail(n, pair)
            if n < 10:
                return u_tail(n - 6, pair)
            return z_tail(n - 10, pair)

        tails = []

        def step():
            if tails:
                try:
                    next(tails[0])
                except StopIteration:
                    tails.pop(0)

        for n in range(14):
            pair = n % 2
            for c, _ in enumerate(self.dense(("in", n), pair)):
                if c % 2 == 1:
                    step()
            while len(tails) > 1:
                step()
            t = tail_of(n, pair)
            next(t)
            tails.append(t)
        while tails:
            step()

    def attention(self, A, heads, q_of, kk_of, v_of, P, pt_tile, out_of, causal, ready, fb_of=None,
                  fb_ready=None, fill=0, late=None):
        k = self.k
        steps = [(h, qt) for h in heads for qt in range(8)]
        g0 = A["n"]
        A["n"] += len(steps)
        n = len(steps)

        def sc(s):
            h, qt = steps[s]
            g = g0 + s
            nk = (qt + 1) * 128 if causal else 1024
            pair = g % 2
            qs = self.wrr(q_of(h))[:, qt * 128:(qt + 1) * 128]
            kh, kl = (self.wrr(i) for i in kk_of(h))
            full = []
            for half in range((nk + 511) // 512):
                b = 2 * pair + half
                c = slice(half * 512, min(nk, half * 512 + 512))
                out = self.ps[pair][:, c]
                diag = causal and c.stop == nk
                k.pe(lambda e, c=c, out=out: e.matmul(out, qs, kh[:, c], start=True, stop=False),
                     self.taken[b] + ready["q", h] + ready["k"], inc=False)
                t = k.pe(lambda e, c=c, out=out, diag=diag: e.matmul(
                    out, qs, kl[:, c], start=False, stop=not diag), (), inc=not diag)
                if diag:
                    o = self.ps[pair][:, nk - 128:nk]
                    t = k.pe(lambda e, o=o: e.matmul(o, self.idr[:, :], self.maskr[:, :],
                                                     start=False, stop=True), self.c)
                full.append(t)
            A["scores", g] = full

        def top(s):
            h, qt = steps[s]
            g = g0 + s
            nk = (qt + 1) * 128 if causal else 1024
            pair = g % 2
            m, den, rd = (self.st[:, 4 * (g % 16) + j:4 * (g % 16) + j + 1] for j in range(3))
            slot = A.get(("exp", g - 16), []) + A.get(("scaled", g - 16), [])
            pw = self.w(P[g % len(P)])[:, 0:nk]
            pfree = A.get(("turned", g - len(P)), A["before"])
            ps = self.ps[pair][:, 0:nk]
            if causal:
                t1 = k.dve(lambda e: e.tensor_tensor_reduce(
                    pw, ps, self.w(fb_of(h))[:, 0:nk], 1.0, -3.0e38, ALU.subtract, ALU.max, m),
                    A["scores", g] + pfree + slot + fb_ready[h])
                t1b = k.dve(lambda e: e.tensor_scalar(m, m, -1.0, None, ALU.mult), [t1])
                A["top", g] = [t1, t1b]
                A["biased", h] = [t1]
            else:
                t1 = k.dve(lambda e: e.tensor_reduce(m, ps, AX, ALU.max, negate=True),
                           A["scores", g] + slot)
                A["top", g] = [t1] + pfree

        def soft(s):
            h, qt = steps[s]
            g = g0 + s
            nk = (qt + 1) * 128 if causal else 1024
            pair = g % 2
            m, den, rd = (self.st[:, 4 * (g % 16) + j:4 * (g % 16) + j + 1] for j in range(3))
            pw = self.w(P[g % len(P)])[:, 0:nk]
            src = pw if causal else self.ps[pair][:, 0:nk]
            t2 = k.act(lambda e: e.activation(pw, src, ACT.Exp, bias=m, scale=1.0,
                                              accum_out=den), A["scores", g] + A["top", g])
            free = A["top", g][0:1] + ([] if causal else [t2])
            for half in range((nk + 511) // 512):
                self.taken[2 * pair + half] = free
            A["exp", g] = [t2]
            t3 = k.dve(lambda e: e.reciprocal(rd, den), A["exp", g])
            t4 = k.pool(lambda e: e.tensor_scalar(pw, pw, rd, 0.0, ALU.mult, ALU.add),
                        A["exp", g] + [t3])
            A["scaled", g] = [t4]

        def turn(s):
            h, qt = steps[s]
            g = g0 + s
            pw = self.w(P[g % len(P)])
            nk = qt + 1 if causal else 8
            hi, lo, lof = pt_tile((g // 2) % 2)
            free = A.get(("product", g // 2 - 2), A["before"])
            par = g % 2 if nk <= 4 else 0
            parts = []
            for half in range((nk + 3) // 4):
                bk = (half + par) % 2
                js = range(4 * half, min(nk, 4 * half + 4))
                for j in js:
                    o = bk * 512 + (j - js[0]) * 128
                    t = k.pe(lambda e, j=j, o=o: e.transpose(
                        self.ps[2][:, o:o + 128], pw[:, j * 128:(j + 1) * 128], self.c_id),
                        A["scaled", g] + self.taken[4 + bk] + self.c, inc=(j == js[-1]))
                src = v3(self.ps[2][:, bk * 512:bk * 512 + len(js) * 128])
                q = slice((qt % 2) * 128, (qt % 2) * 128 + 128)
                dh = hi[:, js[0]:js[-1] + 1, q]
                dl = lo[:, js[0]:js[-1] + 1, q]
                dhf = lof[:, js[0]:js[-1] + 1, q]
                t1 = k.act(lambda e, dh=dh, src=src: e.activation(dh, src, ACT.Copy),
                           [t] + free)
                t2 = k.dve(lambda e, dl=dl, src=src, dhf=dhf: e.tensor_tensor(
                    dl, src, dhf, ALU.subtract), [t, t1] + free)
                self.taken[4 + bk] = [t1, t2]
                parts += [t1, t2]
            A["turned", g] = [t]
            A["parts", g] = parts

        def back(s):
            h, qt = steps[s]
            g = g0 + s
            hi, lo, _ = pt_tile((g // 2) % 2)
            v = self.wrr(v_of(h))
            nk = qt + 1 if causal else 8
            for j in range(nk):
                c0 = 128 if causal and j == qt else 0
                for q, m in enumerate((hi, lo)):
                    last = j == nk - 1 and q == 1
                    t = k.pe(lambda e, j=j, c0=c0, m=m, q=q, last=last: e.matmul(
                        self.ps[3][:, c0:256], v[:, j * 128:(j + 1) * 128], m[:, j, c0:256],
                        start=(j == 0 and q == 0), stop=last),
                        A["parts", g - 1] + A["parts", g] + ready["v"] + self.taken[6], inc=last)
            A["product", g // 2] = [t]
            o_ap, free = out_of(h)
            a = slice(64 * (h % 2), 64 * (h % 2) + 64)
            c = slice((qt // 2) * 256, (qt // 2) * 256 + 256)
            t1 = k.act(lambda e: e.activation(o_ap[a, c], self.ps[3][0:64, 0:256], ACT.Copy),
                       [t] + free)
            t2 = k.dve(lambda e: e.tensor_tensor(o_ap[a, c], self.ps[3][64:128, 0:256], o_ap[a, c],
                                                 ALU.add), [t, t1])
            self.taken[6] = [t2]
            A["out", h] = [t2]

        for s in range(-2, n + 2):
            if s + 2 < n:
                sc(s + 2)
            self.fill(fill)
            if s + 2 < n:
                top(s + 2)
            if late is not None and s + 2 >= n:
                for _ in range(5):
                    next(late, None)
            if 0 <= s < n:
                turn(s)
            if s + 2 < n:
                soft(s + 2)
            if s >= 2 and s % 2 == 0:
                back(s - 1)

    def attend1(self):
        before = self.k.sofar()

        def pt_tile(u):
            a = self.ht[:, u * 4096:u * 4096 + 2048]
            return (v3(a, 256), v3(self.ht[:, u * 4096 + 2048:u * 4096 + 4096], 256),
                    v3(a.bitcast(F32), 256))

        A = self.A1 = {"n": 0, "before": before}
        self.attention(A, range(8), lambda h: h, lambda h: (8, 9) if h < 4 else (10, 11),
                       lambda h: 12 + h // 4, [18, 19, 20, 21], pt_tile,
                       lambda h: (self.htlf(4 + h // 2), before), False, self.ready)

    def mix_out1(self):
        k, d = self.k, self.d
        old = k.sofar()
        xl = [k.dma(self.w(j), d["xT"][j * 128:(j + 1) * 128, :], old) for j in range(8)]
        at = [self.A1["out", 2 * j] + self.A1["out", 2 * j + 1] for j in range(4)]
        acc, acc2, tm, tm2 = old, old, {}, {}
        for j in range(4):
            acc, _ = self.square_add(self.htlf(4 + j), at[j], 1.0, j == 0, 18, acc, 20 + j % 2,
                                     tm.get(j - 2, old))
            tm[j] = acc
        for j in range(4):
            acc2, _ = self.square_add(self.w(14 + j), [self.ready["tok", j]], 1.0, j == 0, 19,
                                      acc2, 10 + j % 2, tm2.get(j - 2, old))
            tm2[j] = acc2
        self.rnorm([18], acc, 1, 1.0 / 512, self.eps, 12, old, 0)
        rt = self.keep(0, 23, old)
        self.rnorm([19], acc2, 1, 1.0 / 512, self.eps, 13, old, 1)
        rt2 = self.keep(1, 22, old)
        tmp, n = {}, 0
        for j in range(4):
            for h in (0, 1):
                tmp[n] = self.norm_split(j, self.htlf(4 + j), at[j], self.p("gao", j), 23, rt,
                                         8 + n % 2, tmp.get(n - 2, old), old, h, None,
                                         "pool" if h else "dve")
                n += 1
        gone = [x for i in range(n) for x in tmp[i]]
        tmp, n = {}, 0
        for h in (0, 1):
            for j in range(4):
                tmp[n] = self.norm_split(4 + j, self.w(14 + j), [self.ready["tok", j]],
                                         self.p("gto", j), 22, rt2, 20 + n % 2,
                                         tmp.get(n - 2, gone + old), gone, h, None,
                                         "pool" if j % 2 else "dve")
                n += 1
        last = [x for i in range(n) for x in tmp[i]]
        acc, tm = last, {}
        self.x = [None] * 8
        for n in range(8):
            pair = n % 4
            self.run(self.dense(("out", n), pair))
            x = self.w(n)
            t = k.dve(lambda e, x=x, n=n, pair=pair: e.scalar_tensor_tensor(
                out=x, in0=self.ps[pair][:, :], scalar=self.mod(2, n), in1=x, op0=ALU.mult,
                op1=ALU.add), self.full(pair) + [xl[n]] + self.mods[2])
            self.took(pair, t)
            self.x[n] = t
            acc, _ = self.square_add(x, [t], 1.0, n == 0, 22, acc, 20 + n % 2,
                                     tm.get(n - 2, last))
            tm[n] = acc
        self.xsum = acc

    def ffn(self):
        k = self.k
        old = k.sofar()
        a = self.col[:, 64:72]
        ta = k.dve(lambda e: e.scalar_tensor_tensor(
            out=a, in0=self.col[:, 40:48], scalar=1.0, in1=self.p("g2", 0, 8), op0=ALU.add,
            op1=ALU.mult), self.mods[4] + old)
        self.rnorm([22], self.xsum, 1, 1.0 / 1024, self.eps, 18, old, 0)
        rt = self.keep(0, 23, old)
        tmp, n = {}, 0
        for h in (0, 1):
            for j in range(8):
                tmp[n] = self.norm_split(j, self.w(j), [self.x[j]], None, 23, rt, 8 + n % 4,
                                         tmp.get(n - 4, old), self.hused, h,
                                         (a[:, j:j + 1], self.mod(3, j), [ta] + self.mods[3]),
                                         "pool" if j % 2 else "dve")
                n += 1
        entry = k.sofar()
        gfree = [entry] * 5
        gparts = [None] * 5
        tfree = [entry, entry]

        def conv(n, pair, i, free):
            x, ps = self.w(i), self.ps[pair]
            w0, w1, w2 = (self.p("wc", 44 * j + n) for j in range(3))
            t1 = k.act(lambda e: e.activation(x, ps[:, :], ACT.Identity, bias=self.p("bc", n),
                                              scale=w1), self.full(pair) + free)
            t2 = k.dve(lambda e: e.scalar_tensor_tensor(
                out=x[:, 1:T], in0=ps[:, 0:T - 1], scalar=w0, in1=x[:, 1:T], op0=ALU.mult,
                op1=ALU.add), self.full(pair) + [t1])
            t3 = k.dve(lambda e: e.scalar_tensor_tensor(
                out=x[:, 0:T - 1], in0=ps[:, 1:T], scalar=w2, in1=x[:, 0:T - 1], op0=ALU.mult,
                op1=ALU.add), [t2])
            self.took(pair, t1, t2, t3)
            return t3

        def pair_up(f):
            slot, u = f % 5, f % 2
            i, j = 18 + 2 * u, 19 + 2 * u
            self.run(self.dense(("up", f), 0))
            ca = conv(f, 0, i, tfree[u])
            self.run(self.dense(("up", NFF + f), 1))
            cb = conv(NFF + f, 1, j, tfree[u])
            x, y = self.w(i), self.w(j)
            t1 = k.act(lambda e: e.activation(x, x, ACT.Silu), [ca])
            t2 = k.dve(lambda e: e.tensor_tensor(x, x, y, ALU.mult), [t1, cb])
            hi, lo = self.wrr(8 + 2 * slot), self.wrr(9 + 2 * slot)
            gparts[slot] = tuple(self.split(x, [t2], hi, lo, gfree[slot], h) for h in (0, 1))
            tfree[u] = gparts[slot][0] + gparts[slot][1] + [t2]

        f0 = 0
        pair_up(0)
        down = 0
        acc1, acc2, tm1, tm2 = entry, entry, {}, {}
        for g, n in enumerate(FG):
            for f in range(f0 + 1, min(f0 + n + 1, NFF)):
                pair_up(f)
            x = [(self.wrr(8 + 2 * (f % 5)), self.wrr(9 + 2 * (f % 5)), gparts[f % 5])
                 for f in range(f0, f0 + n)]
            for j in range(8):
                per = 8 // n
                pair = 2 + down % 2
                down += 1
                self.run(self.dense(("down%d" % g, j // per), pair, kt=n, nk=n,
                                    n0=(j % per) * 128, x=x))
                xr = self.w(j)
                t = k.dve(lambda e, xr=xr, j=j, pair=pair: e.scalar_tensor_tensor(
                    out=xr, in0=self.ps[pair][:, :], scalar=self.mod(5, j), in1=xr, op0=ALU.mult,
                    op1=ALU.add), self.full(pair) + [self.x[j]] + tmp[j] + tmp[8 + j] +
                    self.mods[5])
                self.took(pair, t)
                self.x[j] = t
                if g == len(FG) - 1:
                    if j == 0:
                        acc1 = acc2 = tfree[0] + tfree[1] + [t]
                        done = tfree[0] + tfree[1]
                    acc1, _ = self.square_add(xr, [t], 1.0, j == 0, 22, acc1, 18 + j % 2,
                                              tm1.get(j - 2, done))
                    acc2, _ = self.square_add(xr, [t], self.p("gf", j), j == 0, 23, acc2,
                                              20 + j % 2, tm2.get(j - 2, done))
                    tm1[j], tm2[j] = acc1, acc2
            for f in range(f0, f0 + n):
                gfree[f % 5] = self.lastx
            f0 += n
        self.xsum, self.xgsum = acc1, acc2

    def norms2(self):
        k, d = self.k, self.d
        old = k.sofar()
        self.sums([22], self.xsum, 1, 0)
        self.sums([23], self.xgsum, 1, 1)
        ra, ia, ta = self.rsqrt(0, 1, 1.0 / 1024, self.eps)
        self.spread(ra, ia, ta, 1, 10, old, 0)
        r1t = self.keep(0, 8, old)
        q, iq = self.small()
        q = q[:, 0:8]
        t = k.dve(lambda e: e.tensor_tensor(q, self.ps[1][:, 0:8], ra, ALU.mult),
                  self.made[2] + [ta] + self.sm_read[iq])
        self.taken[2] = [t]
        t = k.dve(lambda e: e.tensor_tensor(q, q, ra, ALU.mult), [t])
        self.sm_read[ia] = self.sm_read[ia] + [t]
        t = k.act(lambda e: e.activation(q, q, ACT.Sqrt, bias=self.eps, scale=1.0 / 1024), [t])
        tq = k.dve(lambda e: e.reciprocal(q, q), [t])
        self.spread(q, iq, tq, 1, 15, old, 1)
        r2t = self.keep(1, 9, old)
        r1 = self.w(8)
        tmp, n = {}, 0
        for h in (0, 1):
            c = slice(h * 512, (h + 1) * 512)
            for j in range(8):
                x = self.w(j)
                t = k.dve(lambda e, x=x, j=j, c=c: e.scalar_tensor_tensor(
                    out=x[:, c], in0=x[:, c], scalar=self.p("gf", j), in1=r1[:, c], op0=ALU.mult,
                    op1=ALU.mult), old + [r1t])
                tmp[n] = self.norm_split(j, x, [t], self.p("gpre", j), 9, r2t, 11 + n % 4,
                                         tmp.get(n - 4, old), self.hused, h, None,
                                         "pool" if j % 2 else "dve")
                n += 1
                if h == 1:
                    self.stored["xres", j] = k.dma(d["xres"][j], x, tmp[j] + [t])

    def rates(self):
        k, d = self.k, self.d
        old = k.sofar()
        self.run(self.dense(("dtf", 0), 2))
        Y, A, E, RW, ONE = (self.w(i) for i in (16, 17, 18, 19, 20))
        r = slice(0, 64)
        ty = k.act(lambda e: e.activation(Y[r, :], self.ps[2][r, :], ACT.Identity,
                                          bias=self.p("rowb")[r, :], scale=1.0),
                   self.full(2) + old)
        self.took(2, ty)
        t = k.act(lambda e: e.activation(A[r, :], Y[r, :], ACT.Abs), [ty] + old)
        ta0 = t
        t = k.act(lambda e: e.activation(E[r, :], A[r, :], ACT.Exp, scale=-1.0), [t] + old)
        te = k.act(lambda e: e.activation(E[r, :], E[r, :], ACT.Ln, bias=self.onev[r, :],
                                          scale=1.0), [t] + self.c)
        an = self.rcol[:, 3:4]
        ta = k.act(lambda e: e.activation(an[0:16, :], self.p("rowa")[0:16, :], ACT.Exp), self.c)
        m1 = k.pool(lambda e: e.memset(RW, 0.0), old)
        m2 = k.pool(lambda e: e.memset(ONE, 1.0), old)
        t1 = k.dve(lambda e: e.scalar_tensor_tensor(
            out=RW[0:16, :], in0=Y[0:16, :], scalar=0.0, in1=E[0:16, :], op0=ALU.max,
            op1=ALU.add), [m1, ty, te])
        t2 = k.dve(lambda e: e.scalar_tensor_tensor(
            out=A[32:48, :], in0=Y[32:48, :], scalar=0.0, in1=E[32:48, :], op0=ALU.min,
            op1=ALU.subtract), [ty, te, ta0])
        t3 = k.dve(lambda e: e.tensor_scalar(A[0:16, :], RW[0:16, :], an[0:16, :], -1.0,
                                             ALU.mult, ALU.mult), [t1, ta, te])
        sc = []
        for c in range(8):
            cc = slice(c * 128, (c + 1) * 128)
            sc.append(k.dve(lambda e, cc=cc: e.tensor_tensor_scan(
                RW[32:48, cc], ONE[0:16, cc], A[0:16, cc], 0.0, ALU.mult, ALU.add), [m1, m2, t3]))
        t4 = k.dve(lambda e: e.tensor_tensor_scan(
            RW[64:80, :], ONE[32:48, :], A[32:48, :], 0.0, ALU.mult, ALU.add), [m1, m2, t2])
        self.rows = [k.dma(d["rows"][0:16], RW[32:48, :], sc),
                     k.dma(d["rows"][16:32], RW[64:80, :], [t4])]
        self.to_tokens(19, [t1, t4] + sc, 2)
        tm = self.keep(2, 23, old)
        self.tm, self.tmt = v3(self.w(23)), [tm]
        t = k.pe(lambda e: e.matmul(self.ps[2][:, 0:128], self.c_last, self.tm[:, :, 32:48],
                                    start=True, stop=True), [tm] + self.taken[4] + self.c)
        t1 = k.act(lambda e: e.activation(self.dec[:, :], self.ps[2][:, 0:128], ACT.Exp), [t])
        t2 = k.dve(lambda e: e.tensor_tensor(
            self.end[:, :].rearrange("p (c h) -> p c h", h=16),
            self.ps[2][:, 0:128].rearrange("p (c h) -> p c h", h=16), self.tm[:, :, 32:48],
            ALU.subtract), [t1, t, tm])
        self.taken[4] = [t1, t2]
        self.endt = [k.act(lambda e: e.activation(self.end[:, :], self.end[:, :], ACT.Exp), [t2])]
        self.dect = [t1]

    def sigmoid_tile(self, name, j, store, pair, i, free, freed):
        k, x = self.k, self.w(i)
        yield from self.dense((name, j), pair)
        t = k.act(lambda e: e.activation(x, self.ps[pair][:, :], ACT.Tanh, scale=0.5),
                  self.full(pair) + free())
        self.took(pair, t)
        t2 = k.pool(lambda e: e.tensor_scalar(x, x, 0.5, 0.5, ALU.mult, ALU.add), [t])
        self.stored[name, j] = k.dma(store[j], x, [t2])
        freed[0] = [self.stored[name, j]]

    def ssm(self):
        k, d, w = self.k, self.d, self.w
        old = k.sofar() + self.rows
        decv = self.dec[:, :].rearrange("p (c h) -> p c h", h=16)
        endv = self.end[:, :].rearrange("p (c h) -> p c h", h=16)
        xdt, xde, prev = (v3(w(i, 2), 256) for i in (6, 8, 10))

        def conv(n, pair, i, free):
            x, ps = w(i), self.ps[pair]
            tap = [self.p("wc2", 16 * j + n) for j in range(4)]
            t = k.act(lambda e: e.activation(x, ps[:, :], ACT.Identity, bias=self.p("bc2", n),
                                             scale=tap[3]), self.full(pair) + free)
            ts = [t]
            for s in (1, 2, 3):
                t = k.dve(lambda e, s=s, x=x: e.scalar_tensor_tensor(
                    out=x[:, s:T], in0=ps[:, 0:T - s], scalar=tap[3 - s], in1=x[:, s:T],
                    op0=ALU.mult, op1=ALU.add), self.full(pair) + [t])
                ts.append(t)
            self.took(pair, *ts)
            return k.act(lambda e: e.activation(x, x, ACT.Silu), [t])

        def zs(j, pair, i, free, out):
            yield from self.dense(("z", j), pair)
            x = w(i)
            t = k.act(lambda e: e.activation(x, self.ps[pair][:, :], ACT.Tanh, scale=0.5),
                      self.full(pair) + free)
            t2 = k.dve(lambda e: e.scalar_tensor_tensor(
                out=x, in0=x, scalar=1.0, in1=self.ps[pair][:, :], op0=ALU.add,
                op1=ALU.mult), [t] + self.full(pair))
            self.took(pair, t, t2)
            out.append(t2)

        def rows_of(hd, i, free):
            return k.dma(w(i), d["rows"][hd:hd + 1, :].partition_broadcast(128), free + self.rows)

        DT = (12, 13, 21, 19)
        last = {x: old for x in ("x0", "x1", "B", "C", "cb", "Bt", "xdt", "xde", "prev", "d0", "d1",
                                 "d2", "d3", "e0", "e1", "y15", "y16", "z17", "z18")}
        gate_free = [old]
        rows = {}

        def decay(g, q):
            hd = 4 * g + q
            x, e_t = w(DT[q]), w((14, 22)[q // 2])
            a = slice(64 * (q % 2), 64 * (q % 2) + 64)
            t = k.act(lambda e: e.activation(e_t[a, :], x[a, :], ACT.Exp),
                      [rows[q]] + last["e%d" % (q // 2)])
            ts = [k.dve(lambda e, c=c: e.tensor_scalar(
                x[:, c * 128:(c + 1) * 128], x[:, c * 128:(c + 1) * 128],
                self.tm[:, c, 32 + hd:33 + hd], 0.0, ALU.subtract, ALU.min),
                [t, rows[q]] + self.tmt) for c in range(8)]
            t2 = k.act(lambda e: e.activation(x, x, ACT.Exp), ts[-1:])
            return t, t2

        def load_rows(g, q, free):
            rows[q] = rows_of(4 * g + q, DT[q], free)

        def norm(g, ty, zt):
            sq = []
            for pr in (0, 1):
                y = w(15 + pr)
                t = k.dve(lambda e, y=y, pr=pr: e.scalar_tensor_tensor(
                    out=y, in0=y, scalar=0.5, in1=w(17 + pr), op0=ALU.mult, op1=ALU.mult),
                    [ty[pr]] + zt[pr])
                last["z%d" % (17 + pr)] = [t]
                ty[pr] = t
                q_i = (4, 5)[pr]
                sq.append(k.act(lambda e, y=y, q_i=q_i: e.activation(w(q_i), y, ACT.Square),
                                [t] + last["cb"] + last["Bt"]))
            yield
            self.sums([4, 5], sq, 1, 2)
            r, i, tr = self.rsqrt(2, 1, 1.0 / 256, self.eps)
            yield
            ts = self.spread(r, i, tr, 1, 4, self.made[4], 2)
            last["cb"] = last["Bt"] = [ts]
            yield
            tk = []
            for pr in (0, 1):
                y = w(15 + pr)
                t = k.dve(lambda e, y=y, pr=pr: e.scalar_tensor_tensor(
                    out=y, in0=y, scalar=self.p("gssm", 2 * g + pr), in1=self.ps[2][:, :],
                    op0=ALU.mult, op1=ALU.mult), [ty[pr], sq[pr]] + self.full(2))
                tk.append(t)
                s = k.dma(d["ys"][2 * g + pr], y, [t])
                self.stored["ys", 2 * g + pr] = s
                last["y%d" % (15 + pr)] = [s]
            self.took(2, *tk)
            yield

        def turn_x(pr, ready, g, tx, te):
            self.to_tokens(pr, [ready], 2 + pr)
            for hh in (0, 1):
                hd = 4 * g + 2 * pr + hh
                o = slice((2 * pr + hh) * 64, (2 * pr + hh) * 64 + 64)
                src = v3(self.ps[2 + pr][:, :])[:, :, 64 * hh:64 * hh + 64]
                t = k.dve(lambda e, o=o, src=src, hd=hd: e.tensor_tensor(
                    xdt[:, :, o], src, self.tm[:, :, hd:hd + 1].broadcast_to([128, 8, 64]),
                    ALU.mult), self.full(2 + pr) + self.tmt + last["xdt"])
                tx.append(t)
                te.append(k.pool(lambda e, o=o, hd=hd: e.tensor_tensor(
                    xde[:, :, o], xdt[:, :, o],
                    endv[:, :, hd:hd + 1].broadcast_to([128, 8, 64]), ALU.mult),
                    [t] + self.endt + last["xde"]))
            self.took(2 + pr, *tx[-2:])

        def run_with(gen, side, at):
            for n, _ in enumerate(gen):
                if n in at:
                    next(side, None)

        side = iter(())
        for q in range(4):
            load_rows(0, q, old)
        for g in range(4):
            run_with(self.dense(("xs", 2 * g), 0), side, (0, 6, 12, 14))
            tx0 = conv(2 * g, 0, 0, last["x0"])
            dec = [decay(g, 0)]
            self.run(self.dense(("xs", 2 * g + 1), 1))
            tx1 = conv(2 * g + 1, 1, 1, last["x1"])
            dec.append(decay(g, 1))
            self.run(self.dense(("B", g), 0))
            tx, te = [], []
            turn_x(0, tx0, g, tx, te)
            tB = conv(8 + g, 0, 2, last["B"])
            dec.append(decay(g, 2))
            turn_x(1, tx1, g, tx, te)
            self.run(self.dense(("C", g), 1))
            tC = conv(12 + g, 1, 3, last["C"])
            tbt = self.to_tokens(2, [tB], 3)
            last["B"] = [tbt]
            tBt = self.keep(3, 5, last["Bt"])
            zt = [[], []]
            self.fillers = [zs(2 * g, 0, 17, last["z17"], zt[0]),
                            zs(2 * g + 1, 1, 18, last["z18"], zt[1])]
            for q in (0, 1):
                self.fillers.append(self.sigmoid_tile("gs", 2 * g + q, d["gs"], q, 20,
                                                      lambda: gate_free[0], gate_free))
            self.fill(5)
            tp = k.pool(lambda e: e.memset(prev[:, 0, :], 0.0), last["prev"])
            pt = [tp]
            cb = []
            for c in range(7):
                bk = 6 + c % 2
                off = (c % 2) * 512
                pp = self.ps[3]
                ts = k.pe(lambda e, c=c, off=off, pp=pp: e.matmul(
                    pp[:, off:off + 256], v3(w(5))[:, c, :], xde[:, c, :], start=True, stop=True),
                    [tBt] + te + self.taken[bk])
                t1 = k.dve(lambda e, c=c, g=g: e.tensor_tensor(
                    v3(prev[:, c + 1, :], 64), v3(prev[:, c, :], 64),
                    decv[:, c, 4 * g:4 * g + 4].unsqueeze(2).broadcast_to([128, 4, 64]),
                    ALU.mult), [tp] + self.dect + last["prev"])
                tp = k.dve(lambda e, c=c, off=off, pp=pp: e.tensor_tensor(
                    prev[:, c + 1, :], pp[:, off:off + 256], prev[:, c + 1, :], ALU.add),
                    [t1, ts])
                self.taken[bk] = [tp]
                pt.append(tp)
                if c == 3:
                    for j in range(8):
                        cc = slice(j * 128, (j + 1) * 128)
                        t = k.pe(lambda e, cc=cc: e.matmul(
                            self.ps[2][:, cc], w(2)[:, cc], w(3)[:, cc], start=True, stop=True),
                            [tB, tC] + self.taken[4 + j // 4], inc=(j % 4 == 3))
                        if j % 4 == 3:
                            self.made[4 + j // 4] = [t]
                    last["B"] = last["B"] + [t]
                    msk = self.mask01.unsqueeze(1).broadcast_to([128, 8, 128])
                    tcb = k.dve(lambda e: e.tensor_tensor(
                        v3(w(4)), v3(self.ps[2][:, :]), msk, ALU.mult),
                        self.full(2) + last["cb"] + self.c)
                    self.took(2, tcb)
                    cb = [k.pool(lambda e, q=q: e.tensor_tensor(
                        w(DT[q]), w(DT[q]), w(4), ALU.mult), [dec[q][1], tcb]) for q in (0, 1)]
                self.fill(2)
            last["Bt"] = last["xde"] = [ts]
            dec.append(decay(g, 3))
            cb += [k.op("dve" if q == 3 else "pool", lambda e, q=q: e.tensor_tensor(
                w(DT[q]), w(DT[q]), w(4), ALU.mult), [dec[q][1], tcb]) for q in (2, 3)]
            last["cb"] = cb
            ty = [None, None]
            for pr in (0, 1):
                y_i = 15 + pr
                y = w(y_i)
                for c in range(8):
                    cc = slice(c * 128, (c + 1) * 128)
                    t = k.pe(lambda e, c=c, cc=cc, pr=pr: e.matmul(
                        self.ps[2][:, cc], prev[:, c, pr * 128:(pr + 1) * 128], w(3)[:, cc],
                        start=True, stop=True), pt + [tC] + self.taken[4 + c // 4],
                        inc=(c % 4 == 3))
                    if c % 4 == 3:
                        self.made[4 + c // 4] = [t]
                last["prev"] = last["C"] = [t]
                self.fill(4)
                for c in range(8):
                    cc = slice(c * 128, (c + 1) * 128)
                    for hh in (0, 1):
                        o = (2 * pr + hh) * 64
                        a = slice(64 * hh, 64 * hh + 64)
                        t = k.pe(lambda e, c=c, cc=cc, o=o, a=a, hh=hh, pr=pr: e.matmul(
                            self.ps[3][a, cc], xdt[:, c, o:o + 64], w(DT[2 * pr + hh])[:, cc],
                            start=True, stop=True),
                            tx + cb[2 * pr:2 * pr + 2] + self.taken[6 + c // 4],
                            inc=(c % 4 == 3 and hh == 1))
                    if c % 4 == 3:
                        self.made[6 + c // 4] = [t]
                last["xdt"] = [t]
                if g < 3:
                    load_rows(g + 1, 2 * pr, [t])
                    load_rows(g + 1, 2 * pr + 1, [t])
                e_t = w((14, 22)[pr])
                t1 = k.dve(lambda e, y=y, e_t=e_t: e.tensor_tensor(y, self.ps[2][:, :], e_t,
                                                                   ALU.mult),
                           self.full(2) + [dec[2 * pr][0], dec[2 * pr + 1][0]] +
                           last["y%d" % y_i])
                self.took(2, t1)
                last["e%d" % pr] = [t1]
                t2 = k.dve(lambda e, y=y: e.tensor_tensor(y, self.ps[3][:, :], y, ALU.add),
                           self.full(3) + [t1])
                self.took(3, t2)
                ty[pr] = k.dve(lambda e, y=y, pr=pr, g=g: e.scalar_tensor_tensor(
                    out=y, in0=w(pr), scalar=self.p("dskip", 2 * g + pr), in1=y, op0=ALU.mult,
                    op1=ALU.add), [t2])
                last["x%d" % pr] = [ty[pr]]
                self.fill(8)
            self.flush()
            side = norm(g, ty, zt)
        for _ in side:
            pass

    def attend2(self):
        k, d, w = self.k, self.d, self.w
        old = k.sofar() + list(self.stored.values())
        A = {"n": 0, "before": old}

        def pt_tile(u):
            r = self.wrr(12 + 4 * u, 4)
            a = r[:, 0:2048]
            return v3(a, 256), v3(r[:, 2048:4096], 256), v3(a.bitcast(F32), 256)

        ready = {}
        state = {"z": old, "o": old, "eight": old}

        def keys(p):
            yield from self.dense(("k", p), 1)
            ts = self.stack(self.ps[1], self.full(1), (2, 4), (3, 5),
                            A.get(("scores", A["n"] - 1), old), 1.0, True)
            self.took(1, *ts)
            ready["k"] = ts

        def silu_z(p, free):
            x = w(23)
            out = []
            for h in (0, 1):
                yield from self.dense(("za", p), 3, halves=(h,), bank=1)
                ps = self.ps[3][:, 512:1024]
                c = slice(h * 512, (h + 1) * 512)
                t = k.act(lambda e, c=c: e.activation(x[:, c], ps, ACT.Tanh, scale=0.5),
                          self.made[7] + free)
                t2 = k.dve(lambda e, c=c: e.scalar_tensor_tensor(
                    out=x[:, c], in0=x[:, c], scalar=1.0, in1=ps, op0=ALU.add, op1=ALU.mult),
                    [t] + self.made[7])
                self.taken[7] = [t, t2]
                out.append(t2)
            state["zt"] = out

        def gate(p, free):
            x = w(8)
            out = []
            for h in (0, 1):
                yield from self.dense(("ga", p), 3, halves=(h,), bank=1)
                ps = self.ps[3][:, 512:1024]
                c = slice(h * 512, (h + 1) * 512)
                t = k.act(lambda e, c=c: e.activation(x[:, c], ps, ACT.Tanh, scale=0.5),
                          self.made[7] + free)
                self.taken[7] = [t]
                out.append(k.pool(lambda e, c=c: e.tensor_scalar(x[:, c], x[:, c], 0.5, 0.5,
                                                                 ALU.mult, ALU.add), [t]))
            self.stored["ga", p] = k.dma(d["ga"][p], x, out)
            state["eight"] = [self.stored["ga", p]]

        late = keys(0)
        for p in range(8):
            fb = {2 * p + hh: [k.dma(w(20 + hh), d["rows"][16 + 2 * p + hh:17 + 2 * p + hh, :]
                                     .partition_broadcast(128),
                                     A.get(("biased", 2 * p - 2 + hh), old) + self.rows)]
                  for hh in (0, 1)}
            self.run(late)
            self.run(self.dense(("q", p), 0))
            ts = self.stack(self.ps[0], self.full(0), (0, 1), (0, 1),
                            A.get(("scores", A["n"] - 1), old), 0.125)
            self.took(0, *ts)
            ready["q", 2 * p] = ready["q", 2 * p + 1] = ts
            self.run(self.dense(("v", p), 3))
            t = self.keep(3, 8, state["eight"])
            tt = self.to_tokens(8, [t], 2)
            ready["v"] = self.stack_v(2, (6, 7), A.get(("product", A["n"] // 2 - 1), old))
            self.fillers = [silu_z(p, state["z"]), gate(p, [tt])]
            late = keys(p + 1) if p < 7 else None
            self.attention(A, (2 * p, 2 * p + 1), lambda h: h % 2,
                           lambda h: (2 + 2 * (h % 2), 3 + 2 * (h % 2)), lambda h: 6 + h % 2,
                           [9, 10, 11], pt_tile, lambda h: (w(22), state["o"]), True, ready,
                           lambda h: 20 + h % 2, fb, 2, self.after_fillers(late))
            t = k.dve(lambda e: e.scalar_tensor_tensor(out=w(22), in0=w(22), scalar=0.5, in1=w(23),
                                                       op0=ALU.mult, op1=ALU.mult),
                      A["out", 2 * p] + A["out", 2 * p + 1] + state["zt"])
            state["z"] = [t]
            self.stored["ya", p] = k.dma(d["ya"][p], w(22), [t])
            state["o"] = [self.stored["ya", p]]

    def after_fillers(self, gen):
        while self.fillers:
            self.fill(1)
            yield
        if gen is not None:
            yield from gen

    def last(self):
        k, d, w = self.k, self.d, self.w
        kept = self.stored
        old = k.sofar() + list(kept.values())
        sp, n = {}, 0
        for j in range(8):
            t = k.dma(w(16 + j % 4), d["ys"][j], sp.get(j - 4, old))
            for h in (0, 1):
                self.hready[h][j] = self.split(w(16 + j % 4), [t], self.hth(j), self.htl(j), old,
                                               h, "pool" if h else "dve")
            sp[j] = self.hready[0][j] + self.hready[1][j]
        x = []
        ys = {}
        ms = {}
        for n in range(8):
            pair = n % 2
            g, i = 20 + n % 2, 18 + n % 2
            tg = k.dma(w(g), d["gs"][n], [kept["m1", n - 2]] if n >= 2 else old)
            ty = k.dma(w(i), d["ya"][n], ys.get(n - 2, sp[6 + n % 2]))
            hi, lo = self.wrr(2 * n), self.wrr(2 * n + 1)
            parts = tuple(self.split(w(i), [ty], hi, lo, old, h, "pool" if h else "dve")
                          for h in (0, 1))
            ys[n] = parts[0] + parts[1]
            x.append((hi, lo, parts))
            self.run(self.dense(("bs", n), pair))
            t = k.dve(lambda e, g=g, pair=pair: e.tensor_tensor(w(g), self.ps[pair][:, :], w(g),
                                                                ALU.mult), self.full(pair) + [tg])
            self.took(pair, t)
            kept["m1", n] = k.dma(d["m1"][n], w(g), [t])
        hfree = self.hused
        done = {}
        for n in range(8):
            pair = 2 + n % 2
            g, m = 20 + n % 2, 22 + n % 2
            tg = k.dma(w(g), d["ga"][n], done[n - 2] if n >= 2 else [kept["m1", 6 + n]])
            tm = k.dma(w(m), d["m1"][n], [kept["m1", n]] + (done[n - 2] if n >= 2 else old))
            self.run(self.dense(("ba", n), pair, x=x))
            t = k.dve(lambda e, g=g, pair=pair: e.tensor_tensor(w(g), self.ps[pair][:, :], w(g),
                                                                ALU.mult), self.full(pair) + [tg])
            self.took(pair, t)
            t = k.dve(lambda e, g=g, m=m: e.tensor_tensor(w(m), w(g), w(m), ALU.add), [t, tm])
            done[n] = [t]
            for h in (0, 1):
                self.hready[h][n] = self.split(w(m), [t], self.hth(n), self.htl(n), hfree, h)
                done[n] = done[n] + self.hready[h][n]
        yused = self.lastx
        free = yused + done[6] + done[7]
        acc, tm = free, {}
        sq = {}
        rs, ot = [], []
        for n in range(8):
            rs.append(k.dma(w(8 + n), d["xres"][n], yused + [kept["xres", n]]))
        for n in range(8):
            pair = n % 4
            self.run(self.dense(("out2", n), pair))
            t = k.act(lambda e, n=n, pair=pair: e.activation(w(n), self.ps[pair][:, :], ACT.Copy),
                      self.full(pair) + yused)
            self.took(pair, t)
            acc, sq[n] = self.square_add(w(n), [t], 1.0, n == 0, 22, acc, 20 + n % 2,
                                         tm.get(n - 2, free))
            tm[n] = acc
            ot.append([t] + sq[n])
        self.rnorm([22], acc, 1, 1.0 / 1024, self.eps, 23, free, 0)
        for n in range(8):
            t = k.dve(lambda e, n=n: e.scalar_tensor_tensor(
                out=w(n), in0=w(n), scalar=self.p("gpost", n), in1=self.ps[0][:, :], op0=ALU.mult,
                op1=ALU.mult), ot[n] + self.full(0))
            t = k.op("pool" if n % 3 == 1 else "dve", lambda e, n=n: e.tensor_tensor(
                w(n), w(n), w(8 + n), ALU.add), [t, rs[n]])
            kept["out", n] = k.dma(d["out"][n * 128:(n + 1) * 128, :], w(n), [t])


def build_program(nc, wst, xT, cst, par, bsb, rope, wsT, out, scratch, phases, stage=99, dbg=None):
    with ExitStack() as ctx:
        d = dict(wst=wst, xT=xT, cst=cst, par=par, bsb=bsb, rope=rope, wsT=wsT, out=out, **scratch)
        K = Kernel(nc, ctx, d)
        for n, ph in enumerate(phases):
            if n < stage:
                ph(K)
        if dbg:
            dbg(K)
        k = K.k
        k.wait("sp", [("d%d" % i, v) for i, v in enumerate(k.dn) if v])
        block = ctx.enter_context(nc.Block())

        @block.tensor
        def _(e):
            for f in k.q["pe"]:
                f(e)

        @block.scalar
        def _(e):
            for f in k.q["act"]:
                f(e)

        @block.vector
        def _(e):
            for f in k.q["dve"]:
                f(e)

        @block.gpsimd
        def _(e):
            for f in k.q["pool"]:
                f(e)

        @block.sync
        def _(e):
            for f in k.q["sp"]:
                f(e)
        return K


PHASES = [Kernel.start, Kernel.norm1, Kernel.project1, Kernel.attend1, Kernel.mix_out1, Kernel.ffn,
          Kernel.norms2, Kernel.rates, Kernel.ssm, Kernel.attend2, Kernel.last]

SCRATCH = {"xres": [8, 128, 1024], "rows": [32, 1024], "gs": [8, 128, 1024], "ga": [8, 128, 1024],
           "ys": [8, 128, 1024], "ya": [8, 128, 1024], "m1": [8, 128, 1024]}


def layout(x, c, w_ada, b_ada, g_norm1, w_in, g_q, g_k, g_tok_v, w_s, b_s, g_attn_out, g_tok_out,
           w_out, g_norm2, w_up, w_conv, b_conv, w_down, g_final, pre_norm_g_2, w_in_2, conv_w_2,
           conv_b_2, dt_bias_2, a_log_2, d_skip_2, ssm_norm_g_2, fgate_b_2, w_branch_ssm_2,
           w_branch_att_2, w_out_2, post_norm_g_2):
    f = np.float32

    def cols(v):
        return np.ascontiguousarray(np.asarray(v).reshape(-1, 128).T)

    wmap = {"in": w_in[0], "out": w_out[0], "up": w_up[0], "bs": w_branch_ssm_2[0],
            "ba": w_branch_att_2[0], "out2": w_out_2[0]}
    wi2 = w_in_2[0]
    o = 0
    for name, width in (("z", 1024), ("xs", 1024), ("B", 512), ("C", 512), ("dt", 16), ("q", 1024),
                        ("k", 1024), ("v", 1024), ("f", 16), ("za", 1024), ("gs", 1024),
                        ("ga", 1024)):
        wmap[name] = wi2[:, o:o + width]
        o += width
    dtf = np.zeros((1024, 128), f)
    dtf[:, 0:16] = wmap["dt"]
    dtf[:, 32:48] = wmap["f"]
    wmap["dtf"] = dtf
    s = plan()
    wst = np.empty((len(s), 128, 1024), f)
    f0 = [sum(FG[:g]) for g in range(len(FG))]
    for i, (kind, name, n) in enumerate(s):
        if kind == "a":
            wst[i] = w_ada[0][n * 128:(n + 1) * 128, name * 1024:(name + 1) * 1024]
        elif name.startswith("down"):
            g = int(name[4:])
            nf = FG[g]
            w = 1024 // nf
            blk = w_down[0][f0[g] * 128:(f0[g] + nf) * 128, n * w:(n + 1) * w]
            wst[i] = blk.reshape(nf, 128, w).transpose(1, 0, 2).reshape(128, 1024)
        else:
            blk = wmap[name][:, n * 128:(n + 1) * 128]
            wst[i] = blk.reshape(8, 128, 128).transpose(1, 0, 2).reshape(128, 1024)
    par = np.zeros((128, NPAR), f)

    def put(name, a):
        par[:, POFF[name]:POFF[name] + a.shape[1]] = a

    put("c", cols(c[0]))
    put("b_ada", cols(b_ada[0]))
    put("g1", cols(g_norm1[0]))
    put("g2", cols(g_norm2[0]))
    put("gf", cols(g_final))
    put("gpre", cols(pre_norm_g_2[0]))
    put("gpost", cols(post_norm_g_2[0]))
    put("gq", np.tile(g_q[0], 2)[:, None])
    put("gk", np.tile(g_k[0], 2)[:, None])
    put("gv", np.tile(g_tok_v[0], 2)[:, None])
    put("gao", cols(g_attn_out[0]))
    put("gto", cols(g_tok_out[0]))
    put("wc", np.concatenate([cols(w_conv[0][j]) for j in range(3)], 1))
    put("bc", cols(b_conv[0]))
    put("wc2", np.concatenate([cols(conv_w_2[0][j]) for j in range(4)], 1))
    put("bc2", cols(conv_b_2[0]))
    rowb = np.zeros((128, 1), f)
    rowb[0:16, 0] = dt_bias_2[0]
    rowb[32:48, 0] = fgate_b_2[0]
    put("rowb", rowb)
    rowa = np.zeros((128, 1), f)
    rowa[0:16, 0] = a_log_2[0]
    put("rowa", rowa)
    put("dskip", cols(np.repeat(d_skip_2[0], 64)))
    put("gssm", cols(ssm_norm_g_2[0]))
    bsb = np.repeat(np.asarray(b_s[0]).reshape(4, 2, 1, 128), 64, axis=2)
    bsb = bsb.reshape(4, 128, 128).transpose(1, 0, 2).reshape(128, 512)
    wsT = np.asarray(w_s[0]).transpose(2, 0, 1).reshape(128, 1024)
    cst, rope = constants()
    return {"wst": wst, "xT": np.ascontiguousarray(np.asarray(x[0]).T), "cst": cst, "par": par,
            "bsb": np.ascontiguousarray(bsb), "rope": rope, "wsT": np.ascontiguousarray(wsT)}


def constants():
    f = np.float32
    i = np.arange(128)
    cst = np.zeros((7, 128, 128), f)
    cst[0] = np.eye(128)
    cst[1] = 1.0
    cst[2] = (i[:, None] // 64 == i[None, :] // 64)
    for m in range(128):
        if m % 32 < 16:
            cst[3, m + 16, m] = -1.0
        else:
            cst[3, m - 16, m] = 1.0
    cst[4, 127, :] = 1.0
    cst[5] = (i[:, None] >= i[None, :])
    cst[6] = (i[:, None] <= i[None, :])
    cst = np.ascontiguousarray(cst.transpose(1, 0, 2).reshape(128, 896))
    t = np.arange(1024)
    inv = np.power(f(10000.0), -np.arange(0, 32, 2, dtype=f) / f(32)).astype(f)
    ar = ((t // 64).astype(f)[:, None] * inv[None, :]).astype(f)
    ac = ((t % 64).astype(f)[:, None] * inv[None, :]).astype(f)
    ang = np.concatenate([ar, ar, ac, ac], 1).T
    ang = np.concatenate([ang, ang], 0)
    rope = np.stack([np.cos(ang), np.sin(ang)]).astype(f)
    return cst, rope


def kernel(**inputs):
    import concourse.bacc as bacc
    from concourse.bass_utils import run_bass_kernel_spmd

    nc = bacc.Bacc("TRN2", target_bir_lowering=False, num_devices=1)
    arrays = layout(**{n: np.asarray(a) for n, a in inputs.items()})
    args = {n: nc.dram_tensor("in_" + n, a.shape, mybir.dt.from_np(a.dtype),
                              kind="ExternalInput").ap() for n, a in arrays.items()}
    out = nc.dram_tensor("out_0", (1024, 1024), F32, kind="ExternalOutput").ap()
    scratch = {n: nc.dram_tensor("scratch_" + n, s, F32, kind="Internal").ap()
               for n, s in SCRATCH.items()}
    build_program(nc, **args, out=out, scratch=scratch, phases=PHASES)
    r = run_bass_kernel_spmd(nc, [{"in_" + n: a for n, a in arrays.items()}], core_ids=[0])
    got = r.results[0]["out_0"]
    return np.ascontiguousarray(np.asarray(got).T)[None]
```

```python
from contextlib import ExitStack

import numpy as np

import concourse.bass as bass
from concourse import mybir

F32 = mybir.dt.float32
F32R = mybir.dt.float32r
ACT = mybir.ActivationFunctionType
ALU = mybir.AluOpType
AX = mybir.AxisListType.X

T = 1024
KT = 8
NFF = 22
EPS = 1e-6
NEG = -1.0e30

PAR = [("c", 8), ("b_ada", 48), ("g1", 8), ("g2", 8), ("gf", 8), ("gpre", 8), ("gpost", 8),
       ("gq", 1), ("gk", 1), ("gv", 1), ("gao", 4), ("gto", 4), ("wc", 132), ("bc", 44),
       ("wc2", 64), ("bc2", 16), ("rowb", 1), ("rowa", 1), ("dskip", 8), ("gssm", 8)]
POFF = {}
NPAR = 0
for _n, _w in PAR:
    POFF[_n] = NPAR
    NPAR += _w

FG = [4, 4, 4, 4, 4, 2]


def plan():
    s = [("a", m, k) for m in (1, 0) for k in range(KT)]
    later = [("a", m, k) for m in (2, 4, 3, 5) for k in range(KT)]
    first = [("w", "in", n) for n in range(14)]
    for n, b in enumerate(first):
        s.append(b)
        if n >= 3:
            s += [later.pop(0) for _ in range(min(3, len(later)))]
    s += later
    s += [("w", "out", n) for n in range(8)]
    f0 = 0
    s += [("w", "up", 0), ("w", "up", NFF)]
    for g, n in enumerate(FG):
        for f in range(f0 + 1, min(f0 + n + 1, NFF)):
            s += [("w", "up", f), ("w", "up", NFF + f)]
        s += [("w", "down%d" % g, b) for b in range(n)]
        f0 += n
    s.append(("w", "dtf", 0))
    for g in range(4):
        s += [("w", "xs", 2 * g), ("w", "xs", 2 * g + 1), ("w", "B", g), ("w", "C", g)]
        s += [("w", "z", 2 * g), ("w", "z", 2 * g + 1), ("w", "gs", 2 * g), ("w", "gs", 2 * g + 1)]
    s.append(("w", "k", 0))
    for p in range(8):
        s += [("w", "q", p), ("w", "v", p), ("w", "za", p), ("w", "ga", p)]
        if p < 7:
            s.append(("w", "k", p + 1))
    for name in ("bs", "ba", "out2"):
        s += [("w", name, n) for n in range(8)]
    return s


class Queues:

    ENG = ("pe", "act", "dve", "pool", "sp")

    def __init__(self, nc, ctx):
        self.q = {e: [] for e in self.ENG}
        self.sem = {e: ctx.enter_context(nc.semaphore("done_" + e)) for e in self.ENG if e != "sp"}
        self.n = {e: 0 for e in self.sem}
        self.seen = {e: {} for e in self.ENG}
        self.ndma = 40
        self.dn = [0] * self.ndma
        self.di = 0
        for i in range(self.ndma):
            self.sem["d%d" % i] = ctx.enter_context(nc.semaphore("dma%d" % i))

    def wait(self, eng, toks):
        for s, v in sorted(toks, key=lambda t: -t[1]):
            if self.seen[eng].get(s, 0) < v:
                self.seen[eng][s] = v
                sem = self.sem[s]
                self.q[eng].append(lambda e, sem=sem, v=v: e.wait_ge(sem, v))

    def op(self, eng, fn, toks=(), inc=True):
        self.wait(eng, toks)
        if not inc:
            self.q[eng].append(fn)
            return None
        self.n[eng] += 1
        sem = self.sem[eng]
        self.q[eng].append(lambda e: fn(e).then_inc(sem, 1))
        return (eng, self.n[eng])

    def pe(self, fn, toks=(), inc=True):
        return self.op("pe", fn, toks, inc)

    def act(self, fn, toks=()):
        return self.op("act", fn, toks)

    def dve(self, fn, toks=()):
        return self.op("dve", fn, toks)

    def pool(self, fn, toks=()):
        return self.op("pool", fn, toks)

    def dma(self, out, in_, toks=()):
        i = self.di % self.ndma
        self.di += 1
        if self.dn[i]:
            self.wait("sp", [("d%d" % i, self.dn[i])])
        self.wait("sp", toks)
        self.dn[i] += 16
        sem = self.sem["d%d" % i]
        self.q["sp"].append(lambda e: e.dma_start(out, in_).then_inc(sem, 16))
        return ("d%d" % i, self.dn[i])

    def sofar(self):
        return [(e, n) for e, n in self.n.items() if n]


def v3(ap, n=128):
    return ap.rearrange("p (c n) -> p c n", n=n)


class Kernel:

    def __init__(self, nc, ctx, d):
        self.nc, self.d = nc, d
        self.k = Queues(nc, ctx)
        base = (nc.sbuf_base + 31) // 32 * 32
        kb = 1024

        def at(name, cols, dt, off):
            return nc.alloc_sbuf_tensor_at(name, [128, cols], dt, offset=base + off)

        self.hl = at("hl", 3 * 2048, F32R, 0)
        self.raw = at("raw", 3 * 1024, F32, 24 * kb)
        self.ht = at("ht", 16 * 1024, F32R, 36 * kb)
        self.htf = at("htf", 16 * 1024, F32, 36 * kb)
        self.wr = at("wr", 24 * 1024, F32R, 100 * kb)
        self.wf = at("wf", 24 * 1024, F32, 100 * kb)
        m = [196 * kb]

        def small(name, cols, dt=F32):
            t = at(name, cols, dt, m[0])
            m[0] += (cols * 4 + 31) // 32 * 32
            assert base + m[0] <= nc.sbuf_usable_end, m[0]
            return t

        self.cst = small("cst", 7 * 128)
        self.par = small("par", NPAR)
        self.bsb = small("bsb", 512)
        self.col = small("col", 128)
        self.st = small("st", 64)
        self.idr = small("idr", 128, F32R)
        self.maskr = small("maskr", 128, F32R)
        self.rcol = small("rcol", 4)
        self.end = small("end", 128)
        self.dec = small("dec", 128)
        self.sm = small("sm", 128)
        self.sm_i = 0
        self.sm_read = [[] for _ in range(8)]
        self.c_id, self.c_one, self.c_bd, self.c_perm, self.c_last, self.c_mask, self.mask01 = (
            self.cst[:, 128 * i:128 * i + 128] for i in range(7))
        self.ps = [nc.alloc_psum_tensor("ps%d" % i, [128, 1024], F32) for i in range(4)]
        self.made = [[] for _ in range(8)]
        self.taken = [[] for _ in range(8)]
        self.hready = [[[] for _ in range(8)] for _ in range(2)]
        self.hused = []
        self.plan = plan()
        self.wlist = [i for i, s in enumerate(self.plan) if s[0] == "w"]
        self.nd = self.np = self.nw = self.wi = 0
        self.cur = None
        self.raw_loaded = [[] for _ in range(3)]
        self.raw_read = [[] for _ in range(3)]
        self.hl_parted = [[] for _ in range(3)]
        self.hl_used = [[] for _ in range(3)]
        self.slot_of = {}
        self.fillers = []
        self.stored = {}
        self.mods = {}
        self.mod_full = None

    def w(self, i, n=1):
        return self.wf[:, i * 1024:(i + n) * 1024]

    def wrr(self, i, n=1):
        return self.wr[:, i * 1024:(i + n) * 1024]

    def p(self, name, j=0, n=1):
        o = POFF[name] + j
        return self.par[:, o:o + n]

    def hth(self, k):
        return self.ht[:, k * 1024:(k + 1) * 1024]

    def htl(self, k):
        return self.ht[:, (8 + k) * 1024:(9 + k) * 1024]

    def htlf(self, k):
        return self.htf[:, (8 + k) * 1024:(9 + k) * 1024]

    def mod(self, m, j):
        return self.col[:, 8 + 8 * m + j:9 + 8 * m + j]

    def full(self, pair):
        return self.made[2 * pair] + self.made[2 * pair + 1]

    def took(self, pair, *toks):
        self.taken[2 * pair] = list(toks)
        self.taken[2 * pair + 1] = list(toks)

    def load_to(self, j):
        while self.nd <= min(j, len(self.plan) - 1):
            i = self.nd
            s = i % 3
            if i >= 16:
                if i - 3 >= self.np:
                    return
                self.raw_loaded[s] = [self.k.dma(self.raw[:, s * 1024:(s + 1) * 1024],
                                                 self.d["wst"][i], self.raw_read[s])]
            self.nd += 1

    def process(self):
        k, i = self.k, self.np
        self.mod_column()
        self.load_to(i)
        kind, name, n = self.plan[i]
        s = i % 3
        src = self.raw[:, s * 1024:(s + 1) * 1024]
        loaded = self.raw_loaded[s]
        if kind == "w":
            u = self.nw % 3
            self.nw += 1
            hi = self.hl[:, u * 2048:u * 2048 + 1024]
            lo = self.hl[:, u * 2048 + 1024:u * 2048 + 2048]
            t1 = k.act(lambda e: e.activation(hi, src, ACT.Copy), loaded + self.hl_used[u])
            t2 = k.pool(lambda e: e.tensor_tensor(lo, src, hi.bitcast(F32), ALU.subtract),
                        loaded + [t1] + self.hl_used[u])
            self.raw_read[s] = [t1, t2]
            self.hl_parted[u] = [t1, t2]
            self.slot_of[i] = u
        else:
            if i < 16:
                src, loaded = self.htf[:, i * 1024:(i + 1) * 1024], self.early[i]
            a = self.w(23)
            cc = self.csilu[:, n:n + 1]
            if n == 0:
                t = k.dve(lambda e: e.tensor_scalar(a, src, cc, None, ALU.mult),
                          loaded + self.silu_c + self.mod_used)
            else:
                t = k.dve(lambda e: e.scalar_tensor_tensor(
                    out=a, in0=src, scalar=cc, in1=a, op0=ALU.mult, op1=ALU.add),
                    loaded + [self.mod_added])
            self.mod_added = t
            if i >= 16:
                self.raw_read[s] = [t]
            if n == KT - 1:
                self.mod_full = name
        self.np += 1
        self.load_to(self.np + 2)

    def ahead(self, i, count=2):
        later = [j for j in self.wlist if j > i][:count]
        last = later[-1] if later else len(self.plan) - 1
        while self.np <= last:
            self.process()

    def mod_column(self):
        m = self.mod_full
        if m is None:
            return
        self.mod_full = None
        k, a = self.k, self.w(23)
        ps = self.ps[3][:, 512:520]
        for j in range(8):
            t = k.pe(lambda e, j=j: e.matmul(ps[:, j:j + 1], a[:, j * 128:(j + 1) * 128],
                                             self.c_one[:, 0:1], start=True, stop=True),
                     [self.mod_added] + self.taken[7] + self.c, inc=(j == 7))
        self.mod_used = [t]
        o = self.col[:, 8 + 8 * m:16 + 8 * m]
        t2 = k.dve(lambda e: e.tensor_tensor(o, ps, self.p("b_ada", 8 * m, 8), ALU.add),
                   [t] + self.c)
        self.taken[7] = [t2]
        self.mods[m] = [t2]

    def fetch(self, key, count=2):
        if self.cur != key:
            i = self.wlist[self.wi]
            assert self.plan[i][1:] == key, (self.plan[i], key)
            self.ahead(i, count)
            self.wi += 1
            self.cur, self.cur_i = key, i
        return self.slot_of[self.cur_i]

    def two(self, key_a, pair_a, key_b, pair_b, first=KT):
        sa, sb = self.fetch(key_a, 1), self.fetch(key_b, 1)
        gens = [self.dense(key, pair, halves=(h,), slot=s)
                for h in (0, 1) for key, pair, s in ((key_a, pair_a, sa), (key_b, pair_b, sb))]
        if first < KT:
            for g in gens:
                for _ in range(first):
                    next(g)
        for a, b in (gens[0:2], gens[2:4]):
            for _ in zip(a, b):
                pass

    def dense(self, key, pair, kt=KT, n0=0, nk=None, x=None, halves=(0, 1), bank=None,
              slot=None):
        k = self.k
        s = self.fetch(key) if slot is None else slot
        nk = nk or kt
        ht = x is None
        for h in halves:
            b = 2 * pair + (h if bank is None else bank)
            out = self.ps[pair][:, (b % 2) * 512:(b % 2 + 1) * 512]
            for j in range(kt):
                w0 = s * 2048 + n0 + j * (1024 // nk)
                wh = self.hl[:, w0:w0 + 128]
                wl = self.hl[:, w0 + 1024:w0 + 1152]
                xh, xl, xr = (self.hth(j), self.htl(j), (self.hready[0][j],
                                                         self.hready[1][j])) if ht else x[j]
                for q, (a, m) in enumerate(((wh, xh), (wh, xl), (wl, xh))):
                    last = j == kt - 1 and q == 2
                    t = k.pe(lambda e, a=a, m=m, q=q, j=j, last=last, out=out, h=h: e.matmul(
                        out, a, m[:, h * 512:(h + 1) * 512], start=(j == 0 and q == 0), stop=last),
                        self.taken[b] + self.hl_parted[s] + xr[h] if q == 0 else (), inc=last)
                if j < kt - 1:
                    yield
            self.made[b] = [t]
            self.hl_used[s] = [t]
            self.lastx = [t]
            if ht:
                self.hused = [t]
            yield

    def run(self, gen):
        for _ in gen:
            pass

    def fill(self, n):
        while n > 0 and self.fillers:
            try:
                next(self.fillers[0])
                n -= 1
            except StopIteration:
                self.fillers.pop(0)

    def flush(self):
        while self.fillers:
            self.fill(1)

    def split(self, src, ready, hi, lo, free, h, eng="dve"):
        k = self.k
        c = slice(h * 512, (h + 1) * 512)
        t1 = k.act(lambda e: e.activation(hi[:, c], src[:, c], ACT.Copy), ready + free)
        t2 = k.op(eng, lambda e: e.tensor_tensor(lo[:, c], src[:, c], hi[:, c].bitcast(F32),
                                                 ALU.subtract), ready + [t1] + free)
        return [t1, t2]

    def square_add(self, x, ready, scale, first, acc_i, acc, tmp_i, tmp_free, eng="dve"):
        k, a, t = self.k, self.w(acc_i), self.w(tmp_i)
        if first:
            t1 = k.act(lambda e: e.activation(a, x, ACT.Square, scale=scale), ready + acc)
            return [t1], [t1]
        t1 = k.act(lambda e: e.activation(t, x, ACT.Square, scale=scale), ready + tmp_free)
        t2 = k.op(eng, lambda e: e.tensor_tensor(a, a, t, ALU.add), acc + [t1])
        return [t2], [t1]

    def times(self, mat, y_i, ready, pair):
        k = self.k
        for h in (0, 1):
            b = 2 * pair + h
            x = self.w(y_i)[:, h * 512:(h + 1) * 512]
            t = k.pe(lambda e, x=x, h=h: e.matmul(self.ps[pair][:, h * 512:(h + 1) * 512], mat, x,
                                                  start=True, stop=True),
                     self.c + ready + self.taken[b])
            self.made[b] = [t]
        return t

    def sums(self, tiles, ready, ncol, pair, bank=0):
        k = self.k
        rhs = self.c_one[:, 0:1] if ncol == 1 else self.cst[:, 256:384:64]
        b = 2 * pair + bank
        for c in range(8):
            for n, i in enumerate(tiles):
                last = c == 7 and n == len(tiles) - 1
                t = k.pe(lambda e, c=c, n=n, i=i: e.matmul(
                    self.ps[pair][:, 512 * bank + c * ncol:512 * bank + (c + 1) * ncol],
                    self.w(i)[:, c * 128:(c + 1) * 128], rhs, start=(n == 0), stop=(n == len(tiles) - 1)),
                    self.c + ready + self.taken[b], inc=last)
        self.made[b] = [t]
        return t

    def small(self):
        i = self.sm_i % 8
        self.sm_i += 1
        return self.sm[:, 16 * i:16 * i + 16], i

    def rsqrt(self, pair, ncol, scale, eps_col, bank=0):
        k, b = self.k, 2 * pair + bank
        r, i = self.small()
        r = r[:, 0:8 * ncol]
        ps = self.ps[pair][:, 512 * bank:512 * bank + 8 * ncol]
        t = k.act(lambda e: e.activation(r, ps, ACT.Sqrt, bias=eps_col, scale=scale), self.made[b] + self.sm_read[i] + self.c)
        self.taken[b] = [t]
        t2 = k.dve(lambda e: e.reciprocal(r, r), [t])
        return r, i, t2

    def spread(self, r, i, ready, ncol, tmp_i, tmp_free, pair):
        k = self.k
        n = 128 // ncol
        tc = k.dve(lambda e: e.tensor_copy(
            self.w(tmp_i).rearrange("p (c n) -> p c n", n=n),
            r.unsqueeze(2).broadcast_to([128, 8 * ncol, n])), [ready] + tmp_free)
        self.sm_read[i] = [tc]
        for h in (0, 1):
            b = 2 * pair + h
            for c in range(4 * h, 4 * h + 4):
                t = k.pe(lambda e, c=c: e.transpose(
                    self.ps[pair][:, c * 128:(c + 1) * 128],
                    self.w(tmp_i)[:, c * 128:(c + 1) * 128], self.c_id),
                    self.c + [tc] + self.taken[b], inc=(c % 4 == 3))
            self.made[b] = [t]
        return t

    def rnorm(self, tiles, ready, ncol, scale, eps_col, tmp_i, tmp_free, pair):
        self.sums(tiles, ready, ncol, pair)
        r, i, t = self.rsqrt(pair, ncol, scale, eps_col)
        return self.spread(r, i, t, ncol, tmp_i, tmp_free, pair)

    def keep(self, pair, r_i, free):
        t = self.k.act(lambda e: e.activation(self.w(r_i), self.ps[pair][:, :], ACT.Copy),
                       self.full(pair) + free)
        self.took(pair, t)
        return t

    def norm_many(self, items, pair, tmps, tmp_free):
        k, r, done, y_of = self.k, self.ps[pair], [], {}
        rt = self.full(pair)
        for n in range(len(items) + 1):
            if n < len(items):
                j, h, src, ready, g, bias, free, eng = items[n]
                c = slice(h * 512, (h + 1) * 512)
                y = self.w(tmps[n % len(tmps)])
                t = k.dve(lambda e, y=y, c=c, src=src, g=g: e.scalar_tensor_tensor(
                    out=y[:, c], in0=src[:, c], scalar=g, in1=r[:, c], op0=ALU.mult,
                    op1=ALU.mult), ready + rt + self.c +
                    (done[n - len(tmps)] if n >= len(tmps) else tmp_free))
                y_of[n] = (y, t)
                t_last = t
            if n > 0:
                j, h, src, ready, g, bias, free, eng = items[n - 1]
                y, t = y_of[n - 1]
                if bias is None:
                    parts = self.split(y, [t], self.hth(j), self.htl(j), free, h, eng)
                else:
                    c = slice(h * 512, (h + 1) * 512)
                    hi, lo = self.hth(j), self.htl(j)
                    t1 = k.act(lambda e, y=y, c=c, hi=hi, bias=bias: e.activation(
                        hi[:, c], y[:, c], ACT.Identity, bias=bias, scale=1.0), [t] + free)
                    t2 = k.dve(lambda e, y=y, c=c, hi=hi, lo=lo, bias=bias:
                               e.scalar_tensor_tensor(
                                   out=lo[:, c], in0=y[:, c], scalar=bias,
                                   in1=hi[:, c].bitcast(F32), op0=ALU.add, op1=ALU.subtract),
                               [t, t1] + free)
                    parts = [t1, t2]
                self.hready[h][j] = parts
                done.append(parts)
        self.took(pair, t_last)
        return done

    def to_tokens(self, y_i, ready, pair):
        k, y = self.k, self.w(y_i)
        for h in (0, 1):
            b = 2 * pair + h
            for c in range(4 * h, 4 * h + 4):
                t = k.pe(lambda e, c=c: e.transpose(self.ps[pair][:, c * 128:(c + 1) * 128],
                                                    y[:, c * 128:(c + 1) * 128], self.c_id),
                         ready + self.c + self.taken[b], inc=(c % 4 == 3))
            self.made[b] = [t]
        return t

    def stack_v(self, pair, tiles, free):
        k = self.k
        ps = v3(self.ps[pair][:, :])
        ta, td = [], []
        for hh in (0, 1):
            dst = v3(self.wrr(tiles[hh]))
            s = slice(64 * hh, 64 * hh + 64)
            ta.append(k.act(lambda e, s=s, dst=dst: e.activation(dst[:, :, 0:64], ps[:, :, s],
                                                                 ACT.Copy), self.full(pair) + free))
        for hh in (0, 1):
            dst = v3(self.wrr(tiles[hh]))
            dstf = v3(self.wrr(tiles[hh]).bitcast(F32))
            s = slice(64 * hh, 64 * hh + 64)
            td.append(k.dve(lambda e, s=s, dst=dst, dstf=dstf: e.tensor_tensor(
                dst[:, :, 64:128], ps[:, :, s], dstf[:, :, 0:64], ALU.subtract),
                self.full(pair) + ta + free))
        self.took(pair, *ta, *td)
        return ta + td

    def stack(self, src, ready, hi, lo, free, scale=1.0, twice=False):
        k = self.k
        ta, td = [], []
        for hh in (0, 1):
            a = slice(64 * hh, 64 * hh + 64)
            o = slice(64 - 64 * hh, 128 - 64 * hh)
            dst = self.wrr(hi[hh])
            for r in (a, o) if twice else (a,):
                ta.append(k.act(lambda e, a=a, r=r, dst=dst: e.activation(
                    dst[r, :], src[a, :], ACT.Copy, scale=scale), ready + free))
        for hh in (0, 1):
            a = slice(64 * hh, 64 * hh + 64)
            o = slice(64 - 64 * hh, 128 - 64 * hh)
            dst, f = self.wrr(lo[hh]), self.wrr(hi[hh]).bitcast(F32)
            for r in (a, o) if twice else (o,):
                td.append(k.dve(lambda e, a=a, r=r, dst=dst, f=f: e.scalar_tensor_tensor(
                    out=dst[r, :], in0=src[a, :], scalar=scale, in1=f[a, :], op0=ALU.mult,
                    op1=ALU.subtract), ready + ta + free))
        return ta + td

    def start(self):
        k, d = self.k, self.d
        self.csilu = self.col[:, 0:8]
        self.mod_used = []
        loads = [k.dma(self.par[:, :], d["par"]), k.dma(self.cst[:, :], d["cst"]),
                 k.dma(self.bsb[:, :], d["bsb"])]
        self.xt, self.early = [], []
        for j in range(8):
            self.xt.append([k.dma(self.w(j), d["xT"][j * 128:(j + 1) * 128, :])])
            self.early.append([k.dma(self.htf[:, j * 1024:(j + 1) * 1024], d["wst"][j])])
        for j in range(8, 16):
            self.early.append([k.dma(self.htf[:, j * 1024:(j + 1) * 1024], d["wst"][j])])
        self.tables = [k.dma(self.w(14), d["rope"][0]), k.dma(self.w(15), d["rope"][1])]
        self.silu_c = [k.act(lambda e: e.activation(self.csilu, self.p("c", 0, 8), ACT.Silu),
                             loads[0:1])]
        self.eps, self.eps64, self.onev = (self.rcol[:, j:j + 1] for j in range(3))
        t1 = k.pool(lambda e: e.memset(self.eps, EPS))
        t2 = k.pool(lambda e: e.memset(self.eps64, 64.0 * EPS))
        t3 = k.pool(lambda e: e.memset(self.onev, 1.0))
        t4 = k.act(lambda e: e.activation(self.idr[:, :], self.c_id, ACT.Copy), loads)
        t5 = k.act(lambda e: e.activation(self.maskr[:, :], self.c_mask, ACT.Copy, scale=-NEG,
                                          bias=NEG), loads)
        self.c = [*loads, t1, t2, t3, t4, t5]

    def norm1(self):
        k = self.k
        acc, adds = [], {}
        for j in range(8):
            acc, _ = self.square_add(self.w(j), self.xt[j], 1.0, j == 0, 8, acc, 9 + j % 2,
                                     adds.get(j - 2, []))
            adds[j] = acc
            if j < 7:
                self.process()
        self.sums([8], acc, 1, 2)
        for _ in range(4):
            self.process()
        r, i, t = self.rsqrt(2, 1, 1.0 / 1024, self.eps)
        self.spread(r, i, t, 1, 11, [], 2)
        while self.np < 16:
            self.process()
        self.mod_column()
        a = self.col[:, 64:72]
        ta = k.dve(lambda e: e.scalar_tensor_tensor(
            out=a, in0=self.col[:, 16:24], scalar=1.0, in1=self.p("g1", 0, 8), op0=ALU.add,
            op1=ALU.mult), self.mods[1] + self.c)
        self.load_to(18)
        free = self.mods[0] + self.mods[1]
        self.ahead(self.wlist[0] - 1)
        bt = self.mods[0] + [ta]
        self.norm_many([(j, h, self.w(j), self.xt[j] + bt, a[:, j:j + 1], self.mod(0, j), free,
                         "dve") for h in (0, 1) for j in range(8)], 2, (18, 19, 20, 21), [])

    def project1(self):
        k, d = self.k, self.d
        COS, SIN = 14, 15
        old = k.sofar()
        tab = self.tables
        yfree, sfree = {0: old, 1: old}, {0: old, 1: old}
        self.f22 = old
        self.rot_used, self.ready = [], {}

        def qk_tail(n, pair):
            g = self.p("gq") if n < 4 else self.p("gk")
            u = n % 2
            y_i, s_i = 18 + 2 * u, 19 + 2 * u
            y, s = self.w(y_i), self.w(s_i)
            ps = self.ps[pair]
            t1 = k.act(lambda e: e.activation(s, ps[:, :], ACT.Square), self.full(pair) + sfree[u])
            t2 = k.act(lambda e: e.activation(y, ps[:, :], ACT.Copy, scale=g),
                       self.full(pair) + yfree[u] + self.c)
            self.took(pair, t1, t2)
            yield
            tsum = self.sums([s_i], [t1], 2, 2)
            trot = self.times(self.c_perm, y_i, [t2], 3)
            r, i, tr = self.rsqrt(2, 2, 1.0 if n < 4 else 1.0 / 64,
                                  self.eps64 if n < 4 else self.eps)
            t4 = k.pool(lambda e: e.tensor_tensor(y, y, self.w(COS), ALU.mult), [t2, trot] + tab)
            yield
            tsp = self.spread(r, i, tr, 2, 22, self.f22, 2)
            self.f22 = [tsp]
            t3 = k.dve(lambda e: e.tensor_tensor(s, self.ps[3][:, :], self.w(SIN), ALU.mult),
                       self.full(3) + tab + [tsum])
            self.took(3, t3)
            t5 = k.dve(lambda e: e.tensor_tensor(y, y, s, ALU.add), [t3, t4])
            t6 = k.dve(lambda e: e.tensor_tensor(y, y, self.ps[2][:, :], ALU.mult),
                       [t5] + self.full(2))
            self.took(2, t6)
            self.rot_used = [t3, t4]
            if n < 4:
                tiles = (2 * n, 2 * n + 1)
                ts = self.stack(y, [t6], tiles, tiles, old)
                self.ready["q", 2 * n] = self.ready["q", 2 * n + 1] = ts
            else:
                ts = self.stack(y, [t6], (8, 10), (9, 11), old, 1.0, True)
                self.ready["k"] = ts
            yfree[u] = ts
            sfree[u] = [t5]
            yield

        def v_tail(n, pair):
            u = n % 2
            y_i = 18 + 2 * u
            t = k.act(lambda e: e.activation(self.w(y_i), self.ps[pair][:, :], ACT.Copy),
                      self.full(pair) + yfree[u])
            self.took(pair, t)
            yield
            tt = self.to_tokens(y_i, [t], 2)
            yfree[u] = [tt]
            yield
            self.ready["v"] = self.stack_v(2, (12, 13), old)
            yield

        def u_tail(n, pair):
            t = k.act(lambda e: e.activation(self.w(14 + n), self.ps[pair][:, :],
                                             ACT.Gelu_apprx_tanh),
                      self.full(pair) + self.rot_used + old)
            self.took(pair, t)
            self.ready["u", n] = t
            yield

        def z_tail(n, pair):
            u = n % 2
            y_i, s_i = 18 + 2 * u, 19 + 2 * u
            y, s, ws = self.w(y_i), self.w(s_i), self.w(22)
            if n == 0:
                self.ws_loaded = k.dma(ws, d["wsT"], self.f22)
            t = k.act(lambda e: e.activation(y, self.ps[pair][:, :], ACT.Gelu_apprx_tanh),
                      self.full(pair) + yfree[u])
            self.took(pair, t)
            t1 = k.act(lambda e: e.activation(s, y, ACT.Square), [t] + sfree[u])
            yield
            tsum = self.sums([s_i], [t1], 2, 2)
            r, i, tr = self.rsqrt(2, 2, 1.0 / 64, self.eps)
            yield
            tsp = self.spread(r, i, tr, 2, s_i, [tsum], 2)
            t2 = k.dve(lambda e: e.scalar_tensor_tensor(
                out=y, in0=y, scalar=self.p("gv"), in1=self.ps[2][:, :], op0=ALU.mult,
                op1=ALU.mult), [t, t1] + self.full(2) + self.c)
            self.took(2, t2)
            yield
            tt = self.to_tokens(y_i, [t2], 3)
            t3 = k.act(lambda e: e.activation(y, self.ps[3][:, :], ACT.Copy),
                       self.full(3) + [tt])
            self.took(3, t3)
            yield
            for c in range(8):
                b = 4 + c // 4
                for hh in (0, 1):
                    hd = 2 * n + hh
                    a = slice(64 * hh, 64 * hh + 64)
                    tm = k.pe(lambda e, c=c, a=a, hd=hd: e.matmul(
                        self.ps[2][a, c * 128:(c + 1) * 128],
                        y[:, c * 128 + a.start:c * 128 + a.stop],
                        ws[:, hd * 128:(hd + 1) * 128], start=True, stop=True),
                        [t3, self.ws_loaded] + self.taken[b], inc=(c % 4 == 3 and hh == 1))
                if c % 4 == 3:
                    self.made[b] = [tm]
            yfree[u] = [tm]
            yield
            bs = self.bsb[:, n * 128:(n + 1) * 128].unsqueeze(1).broadcast_to([128, 8, 128])
            t5 = k.dve(lambda e: e.tensor_tensor(v3(s), v3(self.ps[2][:, :]), bs, ALU.add),
                       self.full(2) + [tsp] + self.c)
            self.took(2, t5)
            x = self.w(14 + n)
            t6 = k.dve(lambda e: e.tensor_tensor(x, x, s, ALU.mult), [t5, self.ready["u", n]])
            sfree[u] = [t6]
            self.ready["tok", n] = t6
            yield

        def tail_of(n, pair):
            if n < 5:
                return qk_tail(n, pair)
            if n == 5:
                return v_tail(n, pair)
            if n < 10:
                return u_tail(n - 6, pair)
            return z_tail(n - 10, pair)

        tails = []

        def step():
            if tails:
                try:
                    next(tails[0])
                except StopIteration:
                    tails.pop(0)

        self.two(("in", 0), 0, ("in", 1), 1)
        for n in range(14):
            pair = n % 2
            if n >= 2:
                slot = self.fetch(("in", n), 1)
                until = self.wlist[self.wi + 1]
                for c, _ in enumerate(self.dense(("in", n), pair, slot=slot)):
                    if c % 2 == 1:
                        step()
                    elif c % 4 == 2 and self.np <= until:
                        self.process()
            while len(tails) > 1:
                step()
            t = tail_of(n, pair)
            next(t)
            tails.append(t)
        while tails:
            step()
        self.mod_column()

    def attention(self, A, heads, q_of, kk_of, v_of, P, pt_tile, out_of, causal, ready, fb_of=None,
                  fb_ready=None, fill=(0,) * 9, late=None, also=None):
        k = self.k
        steps = [(h, qt) for h in heads for qt in range(8)]
        g0 = A["n"]
        A["n"] += len(steps)
        n = len(steps)

        def sc(s):
            h, qt = steps[s]
            g = g0 + s
            nk = (qt + 1) * 128 if causal else 1024
            pair = g % 2
            qs = self.wrr(q_of(h))[:, qt * 128:(qt + 1) * 128]
            kh, kl = (self.wrr(i) for i in kk_of(h))
            full = []
            for half in range((nk + 511) // 512):
                b = 2 * pair + half
                c = slice(half * 512, min(nk, half * 512 + 512))
                out = self.ps[pair][:, c]
                diag = causal and c.stop == nk
                k.pe(lambda e, c=c, out=out: e.matmul(out, qs, kh[:, c], start=True, stop=False),
                     self.taken[b] + ready["q", h] + ready["k"], inc=False)
                t = k.pe(lambda e, c=c, out=out, diag=diag: e.matmul(
                    out, qs, kl[:, c], start=False, stop=not diag), (), inc=not diag)
                if diag:
                    o = self.ps[pair][:, nk - 128:nk]
                    t = k.pe(lambda e, o=o: e.matmul(o, self.idr[:, :], self.maskr[:, :],
                                                     start=False, stop=True), self.c)
                full.append(t)
            A["scores", g] = full

        def top(s):
            h, qt = steps[s]
            g = g0 + s
            nk = (qt + 1) * 128 if causal else 1024
            pair = g % 2
            m, den, rd = (self.st[:, 4 * (g % 16) + j:4 * (g % 16) + j + 1] for j in range(3))
            slot = A.get(("exp", g - 16), []) + A.get(("scaled", g - 16), [])
            pw = self.w(P[g % len(P)])[:, 0:nk]
            pfree = A.get(("turned", g - len(P)), A["before"])
            ps = self.ps[pair][:, 0:nk]
            if causal:
                t1 = k.dve(lambda e: e.tensor_tensor_reduce(
                    pw, ps, self.w(fb_of(h))[:, 0:nk], 1.0, -3.0e38, ALU.subtract, ALU.max, m),
                    A["scores", g] + pfree + slot + fb_ready[h])
                t1b = k.dve(lambda e: e.tensor_scalar(m, m, -1.0, None, ALU.mult), [t1])
                A["top", g] = [t1, t1b]
                A["biased", h] = [t1]
            else:
                t1 = k.dve(lambda e: e.tensor_reduce(m, ps, AX, ALU.max, negate=True),
                           A["scores", g] + slot)
                A["top", g] = [t1] + pfree

        def soft(s):
            h, qt = steps[s]
            g = g0 + s
            nk = (qt + 1) * 128 if causal else 1024
            pair = g % 2
            m, den, rd = (self.st[:, 4 * (g % 16) + j:4 * (g % 16) + j + 1] for j in range(3))
            pw = self.w(P[g % len(P)])[:, 0:nk]
            src = pw if causal else self.ps[pair][:, 0:nk]
            t2 = k.act(lambda e: e.activation(pw, src, ACT.Exp, bias=m, scale=1.0,
                                              accum_out=den), A["scores", g] + A["top", g])
            free = A["top", g][0:1] + ([] if causal else [t2])
            for half in range((nk + 511) // 512):
                self.taken[2 * pair + half] = free
            A["exp", g] = [t2]
            t3 = k.dve(lambda e: e.reciprocal(rd, den), A["exp", g])
            t4 = k.pool(lambda e: e.tensor_scalar(pw, pw, rd, 0.0, ALU.mult, ALU.add),
                        A["exp", g] + [t3])
            A["scaled", g] = [t4]

        def turn(s):
            h, qt = steps[s]
            g = g0 + s
            pw = self.w(P[g % len(P)])
            nk = qt + 1 if causal else 8
            hi, lo, lof = pt_tile((g // 2) % 2)
            free = A.get(("product", g // 2 - 2), A["before"])
            par = g % 2 if nk <= 4 else 0
            parts = []
            for half in range((nk + 3) // 4):
                bk = (half + par) % 2
                js = range(4 * half, min(nk, 4 * half + 4))
                for j in js:
                    o = bk * 512 + (j - js[0]) * 128
                    t = k.pe(lambda e, j=j, o=o: e.transpose(
                        self.ps[2][:, o:o + 128], pw[:, j * 128:(j + 1) * 128], self.c_id),
                        A["scaled", g] + self.taken[4 + bk] + self.c, inc=(j == js[-1]))
                src = v3(self.ps[2][:, bk * 512:bk * 512 + len(js) * 128])
                q = slice((qt % 2) * 128, (qt % 2) * 128 + 128)
                dh = hi[:, js[0]:js[-1] + 1, q]
                dl = lo[:, js[0]:js[-1] + 1, q]
                dhf = lof[:, js[0]:js[-1] + 1, q]
                t1 = k.act(lambda e, dh=dh, src=src: e.activation(dh, src, ACT.Copy),
                           [t] + free)
                t2 = k.dve(lambda e, dl=dl, src=src, dhf=dhf: e.tensor_tensor(
                    dl, src, dhf, ALU.subtract), [t, t1] + free)
                self.taken[4 + bk] = [t1, t2]
                parts += [t1, t2]
            A["turned", g] = [t]
            A["parts", g] = parts

        def back(s):
            h, qt = steps[s]
            g = g0 + s
            hi, lo, _ = pt_tile((g // 2) % 2)
            v = self.wrr(v_of(h))
            nk = qt + 1 if causal else 8
            for j in range(nk):
                c0 = 128 if causal and j == qt else 0
                for q, m in enumerate((hi, lo)):
                    last = j == nk - 1 and q == 1
                    t = k.pe(lambda e, j=j, c0=c0, m=m, q=q, last=last: e.matmul(
                        self.ps[3][:, c0:256], v[:, j * 128:(j + 1) * 128], m[:, j, c0:256],
                        start=(j == 0 and q == 0), stop=last),
                        A["parts", g - 1] + A["parts", g] + ready["v"] + self.taken[6], inc=last)
            A["product", g // 2] = [t]
            o_ap, free = out_of(h)
            a = slice(64 * (h % 2), 64 * (h % 2) + 64)
            c = slice((qt // 2) * 256, (qt // 2) * 256 + 256)
            t1 = k.act(lambda e: e.activation(o_ap[a, c], self.ps[3][0:64, 0:256], ACT.Copy),
                       [t] + free)
            t2 = k.dve(lambda e: e.tensor_tensor(o_ap[a, c], self.ps[3][64:128, 0:256], o_ap[a, c],
                                                 ALU.add), [t, t1])
            self.taken[6] = [t2]
            A["out", h] = [t2]

        for s in range(-2, n + 2):
            if s + 2 < n:
                sc(s + 2)
            self.fill(fill[s % 8] if s >= 0 else fill[8])
            if s + 2 < n:
                top(s + 2)
            if late is not None and s + 2 >= n:
                for _ in range(5):
                    next(late, None)
            if 0 <= s < n:
                turn(s)
            if s + 2 < n:
                soft(s + 2)
            if s >= 2 and s % 2 == 0:
                back(s - 1)
            if also is not None and s in also:
                also[s]()

    def attend1(self):
        k, d = self.k, self.d
        before = self.k.sofar()

        def pt_tile(u):
            a = self.ht[:, u * 4096:u * 4096 + 2048]
            return (v3(a, 256), v3(self.ht[:, u * 4096 + 2048:u * 4096 + 4096], 256),
                    v3(a.bitcast(F32), 256))

        A = self.A1 = {"n": 0, "before": before}
        self.tok, self.att = {"acc": before}, {"acc": before}

        def square_tok(j):
            a, q = self.square_add(self.w(14 + j), [self.ready["tok", j]], 1.0, j == 0, 22,
                                   self.tok["acc"], 23, self.tok["acc"], "pool")
            self.tok["acc"] = a

        def sum_tok():
            self.sums([22], self.tok["acc"], 1, 3, 1)
            self.tok["r"] = self.rsqrt(3, 1, 1.0 / 512, self.eps, 1)

        def square_att(j):
            a, q = self.square_add(self.htlf(4 + j), A["out", 2 * j] + A["out", 2 * j + 1], 1.0,
                                   j == 0, 8, self.att["acc"] + A["scores", 31], 9,
                                   self.att["acc"] + A["scores", 31], "pool")
            self.att["acc"] = a

        def tok_norm():
            seen = A["scores", 63]
            self.xl = [k.dma(self.w(j), d["xT"][j * 128:(j + 1) * 128, :], seen)
                       for j in range(8)]
            r, i, t = self.tok["r"]
            self.spread(r, i, t, 1, 23, self.tok["acc"], 0)
            yield

        also = {4 + 4 * j: (lambda j=j: square_tok(j)) for j in range(4)}
        also[22] = sum_tok
        also.update({36 + 7 * j: (lambda j=j: square_att(j)) for j in range(3)})
        self.attention(A, range(8), lambda h: h, lambda h: (8, 9) if h < 4 else (10, 11),
                       lambda h: 12 + h // 4, [18, 19, 20, 21], pt_tile,
                       lambda h: (self.htlf(4 + h // 2), before), False, self.ready,
                       late=tok_norm(), also=also)

    def mix_out1(self):
        k, A, att = self.k, self.A1, self.att
        at = [A["out", 2 * j] + A["out", 2 * j + 1] for j in range(4)]
        acc, _ = self.square_add(self.htlf(7), at[3], 1.0, False, 8, att["acc"], 9, att["acc"])
        tok = []
        for h in (0, 1):
            tok += self.norm_many([(j, h, self.w(14 + j), [self.ready["tok", j]],
                                    self.p("gto", j), None, A["product", 30],
                                    "pool" if j % 2 else "dve") for j in range(4)],
                                  0, (12, 11) if h == 0 else (10, 19),
                                  A["scores", 63] + A["product", 15] + A["turned", 61])
            if h == 0:
                self.sums([8], acc, 1, 2)
                r, i, t = self.rsqrt(2, 1, 1.0 / 512, self.eps)
        tok = [t for p in tok for t in p]
        sa, sb = self.fetch(("out", 0), 1), self.fetch(("out", 1), 1)
        gens = [self.dense(("out", n), pair, halves=(h,), slot=s)
                for h in (0, 1) for n, pair, s in ((0, 3, sa), (1, 1, sb))]
        for g in gens[0:2]:
            for _ in range(4):
                next(g)
        self.spread(r, i, t, 1, 9, acc, 2)
        for g in gens[2:4]:
            for _ in range(4):
                next(g)
        done = self.norm_many([(4 + j, h, self.htlf(4 + j), at[j], self.p("gao", j), None,
                                A["product", 31], "pool" if j % 2 else "dve")
                               for h in (0, 1) for j in range(4)], 2, (23, 8),
                              tok + self.made[5] + acc + [t])
        for a, b in (gens[0:2], gens[2:4]):
            for _ in zip(a, b):
                pass
        last = [t for p in done for t in p] + tok + A["turned", 62] + A["turned", 63]
        acc, tm = last, {}
        self.x = [None] * 8
        for n in range(8):
            pair = (3, 1, 2, 0)[n % 4]
            if n >= 2:
                self.run(self.dense(("out", n), pair))
            x = self.w(n)
            t = k.dve(lambda e, x=x, n=n, pair=pair: e.scalar_tensor_tensor(
                out=x, in0=self.ps[pair][:, :], scalar=self.mod(2, n), in1=x, op0=ALU.mult,
                op1=ALU.add), self.full(pair) + [self.xl[n]] + self.mods[2])
            self.took(pair, t)
            self.x[n] = t
            acc, _ = self.square_add(x, [t], 1.0, n == 0, 22, acc, 20 + n % 2,
                                     tm.get(n - 2, last))
            tm[n] = acc
        self.xsum = acc

    def ffn(self):
        k = self.k
        old = k.sofar()
        a = self.col[:, 64:72]
        ta = k.dve(lambda e: e.scalar_tensor_tensor(
            out=a, in0=self.col[:, 40:48], scalar=1.0, in1=self.p("g2", 0, 8), op0=ALU.add,
            op1=ALU.mult), self.mods[4] + old)
        self.rnorm([22], self.xsum, 1, 1.0 / 1024, self.eps, 18, old, 2)
        tmp = self.norm_many([(j, h, self.w(j), [self.x[j], ta] + self.mods[3], a[:, j:j + 1],
                               self.mod(3, j), self.hused, "dve")
                              for h in (0, 1) for j in range(8)], 2, (8, 9, 10, 11), old)
        entry = k.sofar()
        gfree = [entry] * 5
        gparts = [None] * 5
        tfree = [entry, entry]

        def conv(n, pair, i, free):
            x, ps = self.w(i), self.ps[pair]
            w0, w1, w2 = (self.p("wc", 44 * j + n) for j in range(3))
            t1 = k.act(lambda e: e.activation(x, ps[:, :], ACT.Identity, bias=self.p("bc", n),
                                              scale=w1), self.full(pair) + free)
            t2 = k.dve(lambda e: e.scalar_tensor_tensor(
                out=x[:, 1:T], in0=ps[:, 0:T - 1], scalar=w0, in1=x[:, 1:T], op0=ALU.mult,
                op1=ALU.add), self.full(pair) + [t1])
            t3 = k.dve(lambda e: e.scalar_tensor_tensor(
                out=x[:, 0:T - 1], in0=ps[:, 1:T], scalar=w2, in1=x[:, 0:T - 1], op0=ALU.mult,
                op1=ALU.add), [t2])
            self.took(pair, t1, t2, t3)
            return t3

        def pair_up(f):
            slot, u = f % 5, f % 2
            i, j = 18 + 2 * u, 19 + 2 * u
            if f == 0:
                self.two(("up", 0), 0, ("up", NFF), 1)
            else:
                self.run(self.dense(("up", f), 0))
            ca = conv(f, 0, i, tfree[u])
            if f > 0:
                self.run(self.dense(("up", NFF + f), 1))
            cb = conv(NFF + f, 1, j, tfree[u])
            x, y = self.w(i), self.w(j)
            t1 = k.act(lambda e: e.activation(x, x, ACT.Silu), [ca])
            t2 = k.dve(lambda e: e.tensor_tensor(x, x, y, ALU.mult), [t1, cb])
            hi, lo = self.wrr(8 + 2 * slot), self.wrr(9 + 2 * slot)
            gparts[slot] = tuple(self.split(x, [t2], hi, lo, gfree[slot], h) for h in (0, 1))
            tfree[u] = gparts[slot][0] + gparts[slot][1] + [t2]

        f0 = 0
        pair_up(0)
        down = 0
        acc1, acc2, tm1, tm2 = entry, entry, {}, {}
        for g, n in enumerate(FG):
            for f in range(f0 + 1, min(f0 + n + 1, NFF)):
                pair_up(f)
            x = [(self.wrr(8 + 2 * (f % 5)), self.wrr(9 + 2 * (f % 5)), gparts[f % 5])
                 for f in range(f0, f0 + n)]
            for j in range(8):
                per = 8 // n
                pair = 2 + down % 2
                down += 1
                self.run(self.dense(("down%d" % g, j // per), pair, kt=n, nk=n,
                                    n0=(j % per) * 128, x=x))
                xr = self.w(j)
                t = k.dve(lambda e, xr=xr, j=j, pair=pair: e.scalar_tensor_tensor(
                    out=xr, in0=self.ps[pair][:, :], scalar=self.mod(5, j), in1=xr, op0=ALU.mult,
                    op1=ALU.add), self.full(pair) + [self.x[j]] + tmp[j] + tmp[8 + j] +
                    self.mods[5])
                self.took(pair, t)
                self.x[j] = t
                if g == len(FG) - 1:
                    if j == 0:
                        acc1 = acc2 = tfree[0] + tfree[1] + [t]
                        done = tfree[0] + tfree[1]
                    acc1, _ = self.square_add(xr, [t], 1.0, j == 0, 22, acc1, 18 + j % 2,
                                              tm1.get(j - 2, done))
                    acc2, _ = self.square_add(xr, [t], self.p("gf", j), j == 0, 23, acc2,
                                              20 + j % 2, tm2.get(j - 2, done),
                                              "pool" if j < 7 else "dve")
                    tm1[j], tm2[j] = acc1, acc2
            for f in range(f0, f0 + n):
                gfree[f % 5] = self.lastx
            f0 += n
        self.xsum, self.xgsum = acc1, acc2

    def norms2(self):
        k, d = self.k, self.d
        old = k.sofar()
        self.sums([22], self.xsum, 1, 0)
        self.sums([23], self.xgsum, 1, 1)
        ra, ia, ta = self.rsqrt(0, 1, 1.0 / 1024, self.eps)
        q, iq = self.small()
        q = q[:, 0:8]
        t = k.dve(lambda e: e.tensor_tensor(q, self.ps[1][:, 0:8], ra, ALU.mult),
                  self.made[2] + [ta] + self.sm_read[iq])
        self.taken[2] = [t]
        t = k.dve(lambda e: e.tensor_tensor(q, q, ra, ALU.mult), [t])
        t = k.act(lambda e: e.activation(q, q, ACT.Sqrt, bias=self.eps, scale=1.0 / 1024), [t])
        t = k.dve(lambda e: e.reciprocal(q, q), [t])
        tq = k.dve(lambda e: e.tensor_tensor(q, q, ra, ALU.mult), [t])
        gg = self.col[:, 72:80]
        tg = k.dve(lambda e: e.tensor_tensor(gg, self.p("gf", 0, 8), self.p("gpre", 0, 8),
                                             ALU.mult), self.c)
        self.spread(q, iq, tq, 1, 15, old, 1)
        self.spread(ra, ia, ta, 1, 10, old, 0)
        self.sm_read[ia] = self.sm_read[ia] + [tq]
        r1t = self.keep(0, 8, old)
        done = self.norm_many([(j, h, self.w(j), [self.x[j], tg], gg[:, j:j + 1], None,
                                self.hused, "dve") for h in (0, 1) for j in range(8)],
                              1, (11, 12, 13, 14), old)
        for h in (0, 1):
            c = slice(h * 512, (h + 1) * 512)
            for j in range(8):
                t = k.pool(lambda e, j=j, c=c: e.tensor_tensor(
                    self.w(j)[:, c], self.w(j)[:, c], self.w(8)[:, c], ALU.mult),
                    done[8 * h + j] + [r1t])
                if h == 1:
                    self.stored["xres", j] = k.dma(d["xres"][j], self.w(j), [t])
        self.two(("dtf", 0), 2, ("xs", 0), 0)

    def rates(self):
        k, d = self.k, self.d
        old = k.sofar()
        Y, A, E, RW, ONE = (self.w(i) for i in (16, 17, 18, 19, 20))
        r = slice(0, 64)
        ty = k.act(lambda e: e.activation(Y[r, :], self.ps[2][r, :], ACT.Identity,
                                          bias=self.p("rowb")[r, :], scale=1.0),
                   self.full(2) + old)
        self.took(2, ty)
        yield
        t = k.act(lambda e: e.activation(A[r, :], Y[r, :], ACT.Abs), [ty] + old)
        ta0 = t
        t = k.act(lambda e: e.activation(E[r, :], A[r, :], ACT.Exp, scale=-1.0), [t] + old)
        te = k.act(lambda e: e.activation(E[r, :], E[r, :], ACT.Ln, bias=self.onev[r, :],
                                          scale=1.0), [t] + self.c)
        an = self.rcol[:, 3:4]
        ta = k.act(lambda e: e.activation(an[0:16, :], self.p("rowa")[0:16, :], ACT.Exp), self.c)
        m1 = k.pool(lambda e: e.memset(RW, 0.0), old)
        m2 = k.pool(lambda e: e.memset(ONE, 1.0), old)
        t1 = k.dve(lambda e: e.scalar_tensor_tensor(
            out=RW[0:16, :], in0=Y[0:16, :], scalar=0.0, in1=E[0:16, :], op0=ALU.max,
            op1=ALU.add), [m1, ty, te])
        t2 = k.dve(lambda e: e.scalar_tensor_tensor(
            out=A[32:48, :], in0=Y[32:48, :], scalar=0.0, in1=E[32:48, :], op0=ALU.min,
            op1=ALU.subtract), [ty, te, ta0])
        t3 = k.dve(lambda e: e.tensor_scalar(A[0:16, :], RW[0:16, :], an[0:16, :], -1.0,
                                             ALU.mult, ALU.mult), [t1, ta, te])
        sc = []
        for c in range(8):
            cc = slice(c * 128, (c + 1) * 128)
            sc.append(k.dve(lambda e, cc=cc: e.tensor_tensor_scan(
                RW[32:48, cc], ONE[0:16, cc], A[0:16, cc], 0.0, ALU.mult, ALU.add), [m1, m2, t3]))
        t4 = k.dve(lambda e: e.tensor_tensor_scan(
            RW[64:80, :], ONE[32:48, :], A[32:48, :], 0.0, ALU.mult, ALU.add), [m1, m2, t2])
        yield
        self.rows = [k.dma(d["rows"][0:16], RW[32:48, :], sc),
                     k.dma(d["rows"][16:32], RW[64:80, :], [t4])]
        self.to_tokens(19, [t1, t4] + sc, 2)
        tm = self.keep(2, 23, old)
        self.tm, self.tmt = v3(self.w(23)), [tm]
        t = k.pe(lambda e: e.matmul(self.ps[2][:, 0:128], self.c_last, self.tm[:, :, 32:48],
                                    start=True, stop=True), [tm] + self.taken[4] + self.c)
        t1 = k.act(lambda e: e.activation(self.dec[:, :], self.ps[2][:, 0:128], ACT.Exp), [t])
        t2 = k.dve(lambda e: e.tensor_tensor(
            self.end[:, :].rearrange("p (c h) -> p c h", h=16),
            self.ps[2][:, 0:128].rearrange("p (c h) -> p c h", h=16), self.tm[:, :, 32:48],
            ALU.subtract), [t1, t, tm])
        self.taken[4] = [t1, t2]
        self.endt = [k.act(lambda e: e.activation(self.end[:, :], self.end[:, :], ACT.Exp), [t2])]
        self.dect = [t1]
        yield

    def sigmoid_tile(self, name, j, store, pair, i, free, freed):
        k, x = self.k, self.w(i)
        yield from self.dense((name, j), pair)
        t = k.act(lambda e: e.activation(x, self.ps[pair][:, :], ACT.Tanh, scale=0.5),
                  self.full(pair) + free())
        self.took(pair, t)
        t2 = k.pool(lambda e: e.tensor_scalar(x, x, 0.5, 0.5, ALU.mult, ALU.add), [t])
        self.stored[name, j] = k.dma(store[j], x, [t2])
        freed[0] = [self.stored[name, j]]

    def ssm(self):
        k, d, w = self.k, self.d, self.w
        old = k.sofar()
        stored = [[self.stored["xres", j]] for j in range(8)]
        decv = self.dec[:, :].rearrange("p (c h) -> p c h", h=16)
        endv = self.end[:, :].rearrange("p (c h) -> p c h", h=16)
        xdt, xde, prev = (v3(w(i, 2), 256) for i in (6, 8, 10))

        def conv(n, pair, i, free):
            x, ps = w(i), self.ps[pair]
            tap = [self.p("wc2", 16 * j + n) for j in range(4)]
            t = k.act(lambda e: e.activation(x, ps[:, :], ACT.Identity, bias=self.p("bc2", n),
                                             scale=tap[3]), self.full(pair) + free)
            ts = [t]
            for s in (1, 2, 3):
                t = k.dve(lambda e, s=s, x=x: e.scalar_tensor_tensor(
                    out=x[:, s:T], in0=ps[:, 0:T - s], scalar=tap[3 - s], in1=x[:, s:T],
                    op0=ALU.mult, op1=ALU.add), self.full(pair) + [t])
                ts.append(t)
            self.took(pair, *ts)
            return k.act(lambda e: e.activation(x, x, ACT.Silu), [t])

        def zs(j, pair, i, free, out):
            yield from self.dense(("z", j), pair)
            x = w(i)
            t = k.act(lambda e: e.activation(x, self.ps[pair][:, :], ACT.Tanh, scale=0.5),
                      self.full(pair) + free)
            t2 = k.dve(lambda e: e.scalar_tensor_tensor(
                out=x, in0=x, scalar=1.0, in1=self.ps[pair][:, :], op0=ALU.add,
                op1=ALU.mult), [t] + self.full(pair))
            self.took(pair, t, t2)
            out.append(t2)

        def rows_of(hd, i, free):
            return k.dma(w(i), d["rows"][hd:hd + 1, :].partition_broadcast(128), free + self.rows)

        DT = (12, 13, 21, 19)
        last = {x: old for x in ("x0", "x1", "B", "C", "cb", "Bt", "xdt", "xde", "prev", "d0", "d1",
                                 "d2", "d3", "e0", "e1", "y15", "y16", "z17", "z18")}
        gate_free = [old]
        rows = {}
        for x, tiles in (("x0", (0,)), ("x1", (1,)), ("B", (2,)), ("C", (3,)), ("cb", (4,)),
                         ("Bt", (5,)), ("xdt", (6, 7))):
            for i in tiles:
                last[x] = last[x] + stored[i]

        def decay(g, q):
            hd = 4 * g + q
            x, e_t = w(DT[q]), w((14, 22)[q // 2])
            a = slice(64 * (q % 2), 64 * (q % 2) + 64)
            t = k.act(lambda e: e.activation(e_t[a, :], x[a, :], ACT.Exp),
                      [rows[q]] + last["e%d" % (q // 2)])
            ts = [k.dve(lambda e, c=c: e.tensor_scalar(
                x[:, c * 128:(c + 1) * 128], x[:, c * 128:(c + 1) * 128],
                self.tm[:, c, 32 + hd:33 + hd], 0.0, ALU.subtract, ALU.min),
                [t, rows[q]] + self.tmt) for c in range(8)]
            t2 = k.act(lambda e: e.activation(x, x, ACT.Exp), ts[-1:])
            return t, t2

        def load_rows(g, q, free):
            rows[q] = rows_of(4 * g + q, DT[q], free)

        def norm(g, ty, zt):
            sq = []
            for pr in (0, 1):
                y = w(15 + pr)
                t = k.dve(lambda e, y=y, pr=pr: e.scalar_tensor_tensor(
                    out=y, in0=y, scalar=0.5, in1=w(17 + pr), op0=ALU.mult, op1=ALU.mult),
                    [ty[pr]] + zt[pr])
                last["z%d" % (17 + pr)] = [t]
                ty[pr] = t
                q_i = (4, 5)[pr]
                sq.append(k.act(lambda e, y=y, q_i=q_i: e.activation(w(q_i), y, ACT.Square),
                                [t] + last["cb"] + last["Bt"]))
            yield
            self.sums([4, 5], sq, 1, 2)
            r, i, tr = self.rsqrt(2, 1, 1.0 / 256, self.eps)
            yield
            ts = self.spread(r, i, tr, 1, 4, self.made[4], 2)
            last["cb"] = last["Bt"] = [ts]
            yield
            tk = []
            for pr in (0, 1):
                y = w(15 + pr)
                t = k.dve(lambda e, y=y, pr=pr: e.scalar_tensor_tensor(
                    out=y, in0=y, scalar=self.p("gssm", 2 * g + pr), in1=self.ps[2][:, :],
                    op0=ALU.mult, op1=ALU.mult), [ty[pr], sq[pr]] + self.full(2))
                tk.append(t)
                s = k.dma(d["ys"][2 * g + pr], y, [t])
                self.stored["ys", 2 * g + pr] = s
                last["y%d" % (15 + pr)] = [s]
            self.took(2, *tk)
            yield

        def turn_x(pr, ready, g, tx, te):
            self.to_tokens(pr, [ready], 2 + pr)
            for hh in (0, 1):
                hd = 4 * g + 2 * pr + hh
                o = slice((2 * pr + hh) * 64, (2 * pr + hh) * 64 + 64)
                src = v3(self.ps[2 + pr][:, :])[:, :, 64 * hh:64 * hh + 64]
                t = k.dve(lambda e, o=o, src=src, hd=hd: e.tensor_tensor(
                    xdt[:, :, o], src, self.tm[:, :, hd:hd + 1].broadcast_to([128, 8, 64]),
                    ALU.mult), self.full(2 + pr) + self.tmt + last["xdt"])
                tx.append(t)
                te.append(k.pool(lambda e, o=o, hd=hd: e.tensor_tensor(
                    xde[:, :, o], xdt[:, :, o],
                    endv[:, :, hd:hd + 1].broadcast_to([128, 8, 64]), ALU.mult),
                    [t] + self.endt + last["xde"]))
            self.took(2 + pr, *tx[-2:])

        def run_with(gen, side, at):
            for n, _ in enumerate(gen):
                if n in at:
                    next(side, None)

        zero = k.pool(lambda e: e.memset(prev[:, 0, :], 0.0), old)
        side = self.rates()
        for g in range(4):
            if g == 0:
                next(side)
                tx0 = conv(0, 0, 0, last["x0"])
                self.ahead(self.cur_i)
                next(side)
                self.run(self.dense(("xs", 1), 1))
                tx1 = conv(1, 1, 1, last["x1"])
                self.run(self.dense(("B", 0), 0))
                next(side)
                tB = conv(8, 0, 2, last["B"])
                late = k.sofar() + self.rows
                for x in ("d3", "y15", "y16", "z17", "z18"):
                    last[x] = late
                gate_free[0] = late
                for q in range(4):
                    load_rows(0, q, late if q == 3 else old)
                dec = [decay(0, 0), decay(0, 1)]
            else:
                run_with(self.dense(("xs", 2 * g), 0), side, (0, 6, 12, 14))
                tx0 = conv(2 * g, 0, 0, last["x0"])
                dec = [decay(g, 0)]
                self.run(self.dense(("xs", 2 * g + 1), 1))
                tx1 = conv(2 * g + 1, 1, 1, last["x1"])
                dec.append(decay(g, 1))
                self.run(self.dense(("B", g), 0))
                tB = conv(8 + g, 0, 2, last["B"])
            tx, te = [], []
            turn_x(0, tx0, g, tx, te)
            turn_x(1, tx1, g, tx, te)
            if g == 0:
                dec.append(decay(g, 2))
            self.run(self.dense(("C", g), 1))
            zt = [[], []]
            self.fillers = [zs(2 * g, 0, 17, last["z17"], zt[0]),
                            zs(2 * g + 1, 1, 18, last["z18"], zt[1])]
            for q in (0, 1):
                self.fillers.append(self.sigmoid_tile("gs", 2 * g + q, d["gs"], q, 20,
                                                      lambda: gate_free[0], gate_free))
            if g == 0:
                self.fill(4)
            else:
                tC = conv(12 + g, 1, 3, last["C"])
            tbt = self.to_tokens(2, [tB], 3)
            last["B"] = [tbt]
            tBt = self.keep(3, 5, last["Bt"])
            if g == 0:
                tC = conv(12, 1, 3, last["C"])
            else:
                dec.append(decay(g, 2))
            self.fill(7 if g == 0 else 8)
            tp = zero
            pt = [tp]
            cb = []
            for c in range(7):
                bk = 6 + c % 2
                off = (c % 2) * 512
                pp = self.ps[3]
                ts = k.pe(lambda e, c=c, off=off, pp=pp: e.matmul(
                    pp[:, off:off + 256], v3(w(5))[:, c, :], xde[:, c, :], start=True, stop=True),
                    [tBt] + te + self.taken[bk])
                t1 = k.dve(lambda e, c=c, g=g: e.tensor_tensor(
                    v3(prev[:, c + 1, :], 64), v3(prev[:, c, :], 64),
                    decv[:, c, 4 * g:4 * g + 4].unsqueeze(2).broadcast_to([128, 4, 64]),
                    ALU.mult), [tp] + self.dect + last["prev"])
                tp = k.dve(lambda e, c=c, off=off, pp=pp: e.tensor_tensor(
                    prev[:, c + 1, :], pp[:, off:off + 256], prev[:, c + 1, :], ALU.add),
                    [t1, ts])
                self.taken[bk] = [tp]
                pt.append(tp)
                if c == 3:
                    for j in range(8):
                        cc = slice(j * 128, (j + 1) * 128)
                        t = k.pe(lambda e, cc=cc: e.matmul(
                            self.ps[2][:, cc], w(2)[:, cc], w(3)[:, cc], start=True, stop=True),
                            [tB, tC] + self.taken[4 + j // 4], inc=(j % 4 == 3))
                        if j % 4 == 3:
                            self.made[4 + j // 4] = [t]
                    last["B"] = last["B"] + [t]
                    msk = self.mask01.unsqueeze(1).broadcast_to([128, 8, 128])
                    tcb = k.dve(lambda e: e.tensor_tensor(
                        v3(w(4)), v3(self.ps[2][:, :]), msk, ALU.mult),
                        self.full(2) + last["cb"] + self.c)
                    self.took(2, tcb)
                    cb = [k.pool(lambda e, q=q: e.tensor_tensor(
                        w(DT[q]), w(DT[q]), w(4), ALU.mult), [dec[q][1], tcb]) for q in (0, 1)]
                self.fill(2)
            last["Bt"] = last["xde"] = [ts]
            dec.append(decay(g, 3))
            cb += [k.op("dve" if q == 3 else "pool", lambda e, q=q: e.tensor_tensor(
                w(DT[q]), w(DT[q]), w(4), ALU.mult), [dec[q][1], tcb]) for q in (2, 3)]
            last["cb"] = cb
            ty = [None, None]
            for pr in (0, 1):
                y_i = 15 + pr
                y = w(y_i)
                for c in range(8):
                    cc = slice(c * 128, (c + 1) * 128)
                    t = k.pe(lambda e, c=c, cc=cc, pr=pr: e.matmul(
                        self.ps[2][:, cc], prev[:, c, pr * 128:(pr + 1) * 128], w(3)[:, cc],
                        start=True, stop=True), pt + [tC] + self.taken[4 + c // 4],
                        inc=(c % 4 == 3))
                    if c % 4 == 3:
                        self.made[4 + c // 4] = [t]
                last["prev"] = last["C"] = [t]
                self.fill(4)
                for c in range(8):
                    cc = slice(c * 128, (c + 1) * 128)
                    for hh in (0, 1):
                        o = (2 * pr + hh) * 64
                        a = slice(64 * hh, 64 * hh + 64)
                        t = k.pe(lambda e, c=c, cc=cc, o=o, a=a, hh=hh, pr=pr: e.matmul(
                            self.ps[3][a, cc], xdt[:, c, o:o + 64], w(DT[2 * pr + hh])[:, cc],
                            start=True, stop=True),
                            tx + cb[2 * pr:2 * pr + 2] + self.taken[6 + c // 4],
                            inc=(c % 4 == 3 and hh == 1))
                    if c % 4 == 3:
                        self.made[6 + c // 4] = [t]
                last["xdt"] = [t]
                if g < 3:
                    load_rows(g + 1, 2 * pr, [t])
                    load_rows(g + 1, 2 * pr + 1, [t])
                e_t = w((14, 22)[pr])
                t1 = k.dve(lambda e, y=y, e_t=e_t: e.tensor_tensor(y, self.ps[2][:, :], e_t,
                                                                   ALU.mult),
                           self.full(2) + [dec[2 * pr][0], dec[2 * pr + 1][0]] +
                           last["y%d" % y_i])
                self.took(2, t1)
                last["e%d" % pr] = [t1]
                t2 = k.dve(lambda e, y=y: e.tensor_tensor(y, self.ps[3][:, :], y, ALU.add),
                           self.full(3) + [t1])
                self.took(3, t2)
                ty[pr] = k.dve(lambda e, y=y, pr=pr, g=g: e.scalar_tensor_tensor(
                    out=y, in0=w(pr), scalar=self.p("dskip", 2 * g + pr), in1=y, op0=ALU.mult,
                    op1=ALU.add), [t2])
                last["x%d" % pr] = [ty[pr]]
                self.fill(8)
            self.flush()
            side = norm(g, ty, zt)
        for _ in side:
            pass

    def attend2(self):
        k, d, w = self.k, self.d, self.w
        old = k.sofar() + list(self.stored.values())
        A = self.A2 = {"n": 0, "before": old}

        def pt_tile(u):
            r = self.wrr(12 + 4 * u, 4)
            a = r[:, 0:2048]
            return v3(a, 256), v3(r[:, 2048:4096], 256), v3(a.bitcast(F32), 256)

        FILL, FILL7 = (2, 2, 2, 2, 2, 2, 2, 2, 2), (3, 3, 3, 3, 3, 3, 3, 3, 3)
        ready = {}
        state = {"z": old, "o": old, "eight": old}

        def keys(p):
            yield from self.dense(("k", p), 1)
            ts = self.stack(self.ps[1], self.full(1), (2, 4), (3, 5),
                            A.get(("scores", A["n"] - 1), old), 1.0, True)
            self.took(1, *ts)
            ready["k"] = ts

        def silu_z(p, free):
            x = w(23)
            out = []
            for h in (0, 1):
                yield from self.dense(("za", p), 3, halves=(h,), bank=1)
                ps = self.ps[3][:, 512:1024]
                c = slice(h * 512, (h + 1) * 512)
                t = k.act(lambda e, c=c: e.activation(x[:, c], ps, ACT.Tanh, scale=0.5),
                          self.made[7] + free)
                t2 = k.dve(lambda e, c=c: e.scalar_tensor_tensor(
                    out=x[:, c], in0=x[:, c], scalar=1.0, in1=ps, op0=ALU.add, op1=ALU.mult),
                    [t] + self.made[7])
                self.taken[7] = [t, t2]
                out.append(t2)
                yield
                yield
            state["zt"] = out

        def gate(p, free):
            x = w(8)
            out = []
            for h in (0, 1):
                yield from self.dense(("ga", p), 3, halves=(h,), bank=1)
                ps = self.ps[3][:, 512:1024]
                c = slice(h * 512, (h + 1) * 512)
                t = k.act(lambda e, c=c: e.activation(x[:, c], ps, ACT.Tanh, scale=0.5),
                          self.made[7] + free)
                self.taken[7] = [t]
                out.append(k.pool(lambda e, c=c: e.tensor_scalar(x[:, c], x[:, c], 0.5, 0.5,
                                                                 ALU.mult, ALU.add), [t]))
                if h == 0:
                    yield
            self.stored["ga", p] = k.dma(d["ga"][p], x, out)
            state["eight"] = [self.stored["ga", p]]

        late = keys(0)
        for p in range(8):
            fb = {2 * p + hh: [k.dma(w(20 + hh), d["rows"][16 + 2 * p + hh:17 + 2 * p + hh, :]
                                     .partition_broadcast(128),
                                     A.get(("biased", 2 * p - 2 + hh), old) + self.rows)]
                  for hh in (0, 1)}
            self.run(late)
            self.run(self.dense(("q", p), 0))
            ts = self.stack(self.ps[0], self.full(0), (0, 1), (0, 1),
                            A.get(("scores", A["n"] - 1), old), 0.125)
            self.took(0, *ts)
            ready["q", 2 * p] = ready["q", 2 * p + 1] = ts
            self.run(self.dense(("v", p), 3))
            t = self.keep(3, 8, state["eight"])
            tt = self.to_tokens(8, [t], 2)
            ready["v"] = self.stack_v(2, (6, 7), A.get(("product", A["n"] // 2 - 1), old))
            self.fillers = [silu_z(p, state["z"]), gate(p, [tt])]
            late, also = None, None
            if p < 7:
                late = self.after_fillers(keys(p + 1))
            else:
                ys = self.load_ys()
                also = {s: (lambda: next(ys)) for s in (11, 12, 13, 14)}
                also[10] = lambda: (self.flush(), next(ys))
            self.attention(A, (2 * p, 2 * p + 1), lambda h: h % 2,
                           lambda h: (2 + 2 * (h % 2), 3 + 2 * (h % 2)), lambda h: 6 + h % 2,
                           [9, 10, 11], pt_tile, lambda h: (w(22), state["o"]), True, ready,
                           lambda h: 20 + h % 2, fb, FILL if p < 7 else FILL7,
                           late, also)
            t = k.dve(lambda e: e.scalar_tensor_tensor(out=w(22), in0=w(22), scalar=0.5, in1=w(23),
                                                       op0=ALU.mult, op1=ALU.mult),
                      A["out", 2 * p] + A["out", 2 * p + 1] + state["zt"])
            state["z"] = [t]
            self.stored["ya", p] = k.dma(d["ya"][p], w(22), [t])
            state["o"] = [self.stored["ya", p]]

    def after_fillers(self, gen):
        while self.fillers:
            self.fill(1)
            yield
        if gen is not None:
            yield from gen

    def load_ys(self):
        k = self.k
        free = self.hused
        loads = [k.dma(self.htlf(j), self.d["ys"][j], free + [self.stored["ys", j]])
                 for j in range(8)]
        yield
        for j in range(8):
            for h in (0, 1):
                self.hready[h][j] = self.split(self.htlf(j), [loads[j]], self.hth(j),
                                               self.htl(j), free, h, "pool" if h else "dve")
            if j % 2 == 1:
                yield

    def last(self):
        k, d, w = self.k, self.d, self.w
        kept = self.stored
        old = k.sofar() + list(kept.values())
        x = []
        loads, gates = [], []

        def load(n):
            if n < 8:
                loads.append(k.dma(w(2 * n + 1), d["ya"][n], old))
                gates.append(k.dma(w(20 + n % 4), d["gs"][n],
                                   [kept["m1", n - 4]] if n >= 4 else old))

        for n in range(3):
            load(n)
        self.two(("bs", 0), 0, ("bs", 1), 1)
        for n in range(8):
            pair = n % 2
            g, i = 20 + n % 4, 2 * n + 1
            tg = gates[n]
            if n > 1:
                self.run(self.dense(("bs", n), pair))
            hi, lo = self.wrr(2 * n), self.wrr(2 * n + 1)
            parts = tuple(self.split(w(i), [loads[n]], hi, lo, old, h, "pool" if h else "dve")
                          for h in (0, 1))
            x.append((hi, lo, parts))
            t = k.dve(lambda e, g=g, pair=pair: e.tensor_tensor(w(g), self.ps[pair][:, :], w(g),
                                                                ALU.mult), self.full(pair) + [tg])
            self.took(pair, t)
            kept["m1", n] = k.dma(d["m1"][n], w(g), [t])
            load(n + 3)
        hfree = self.hused
        done = {}
        for n in range(8):
            pair = 2 + n % 2
            g, m = 20 + n % 2, 22 + n % 2
            before = done[n - 2] if n >= 2 else [kept["m1", j] for j in (4, 5, 6, 7)]
            tg = k.dma(w(g), d["ga"][n], before)
            tm = k.dma(w(m), d["m1"][n], [kept["m1", n]] + before)
            self.run(self.dense(("ba", n), pair, x=x))
            t = k.dve(lambda e, g=g, pair=pair: e.tensor_tensor(w(g), self.ps[pair][:, :], w(g),
                                                                ALU.mult), self.full(pair) + [tg])
            self.took(pair, t)
            t = k.dve(lambda e, g=g, m=m: e.tensor_tensor(w(m), w(g), w(m), ALU.add), [t, tm])
            done[n] = [t]
            for h in (0, 1):
                self.hready[h][n] = self.split(w(m), [t], self.hth(n), self.htl(n), hfree, h)
                done[n] = done[n] + self.hready[h][n]
        yused = self.lastx
        free = yused + done[6] + done[7]
        acc, tm = free, {}
        sq = {}
        rs, ot = [], []
        for n in range(8):
            t = k.dma(w(8 + n), d["xres"][n], yused + [kept["xres", n]])
            rs.append(k.pool(lambda e, n=n: e.tensor_scalar(w(8 + n), w(8 + n), self.p("gf", n),
                                                            0.0, ALU.mult, ALU.add), [t]))
        for n in range(8):
            pair = n % 4
            self.run(self.dense(("out2", n), pair))
            t = k.act(lambda e, n=n, pair=pair: e.activation(
                w(n), self.ps[pair][:, :], ACT.Copy, scale=self.p("gpost", n)),
                self.full(pair) + yused)
            acc, sq[n] = self.square_add(self.ps[pair][:, :], self.full(pair), 1.0, n == 0, 22,
                                         acc, 20 + n % 2, tm.get(n - 2, free))
            self.took(pair, t, *sq[n])
            tm[n] = acc
            ot.append([t])
        self.rnorm([22], acc, 1, 1.0 / 1024, self.eps, 23, free, 0)
        rt = self.keep(0, 22, acc + self.made[0])
        order = [(0, "pool"), (1, "dve"), (2, "dve"), (3, "dve"), (4, "pool"), (5, "dve"),
                 (6, "dve"), (7, "dve")]
        for n, eng in order:
            t = k.op(eng, lambda e, n=n: e.tensor_tensor(w(n), w(n), w(22), ALU.mult),
                     ot[n] + [rt])
            t = k.op(eng, lambda e, n=n: e.tensor_tensor(w(n), w(n), w(8 + n), ALU.add),
                     [t, rs[n]])
            kept["out", n] = k.dma(d["out"][n * 128:(n + 1) * 128, :], w(n), [t])


def build_program(nc, wst, xT, cst, par, bsb, rope, wsT, out, scratch, phases):
    with ExitStack() as ctx:
        d = dict(wst=wst, xT=xT, cst=cst, par=par, bsb=bsb, rope=rope, wsT=wsT, out=out, **scratch)
        K = Kernel(nc, ctx, d)
        for ph in phases:
            ph(K)
        k = K.k
        k.wait("sp", [("d%d" % i, v) for i, v in enumerate(k.dn) if v])
        block = ctx.enter_context(nc.Block())

        @block.tensor
        def _(e):
            for f in k.q["pe"]:
                f(e)

        @block.scalar
        def _(e):
            for f in k.q["act"]:
                f(e)

        @block.vector
        def _(e):
            for f in k.q["dve"]:
                f(e)

        @block.gpsimd
        def _(e):
            for f in k.q["pool"]:
                f(e)

        @block.sync
        def _(e):
            for f in k.q["sp"]:
                f(e)
        return K


PHASES = [Kernel.start, Kernel.norm1, Kernel.project1, Kernel.attend1, Kernel.mix_out1, Kernel.ffn,
          Kernel.norms2, Kernel.ssm, Kernel.attend2, Kernel.last]

SCRATCH = {"xres": [8, 128, 1024], "rows": [32, 1024], "gs": [8, 128, 1024], "ga": [8, 128, 1024],
           "ys": [8, 128, 1024], "ya": [8, 128, 1024], "m1": [8, 128, 1024]}


def layout(x, c, w_ada, b_ada, g_norm1, w_in, g_q, g_k, g_tok_v, w_s, b_s, g_attn_out, g_tok_out,
           w_out, g_norm2, w_up, w_conv, b_conv, w_down, g_final, pre_norm_g_2, w_in_2, conv_w_2,
           conv_b_2, dt_bias_2, a_log_2, d_skip_2, ssm_norm_g_2, fgate_b_2, w_branch_ssm_2,
           w_branch_att_2, w_out_2, post_norm_g_2):
    f = np.float32

    def cols(v):
        return np.ascontiguousarray(np.asarray(v).reshape(-1, 128).T)

    wmap = {"in": w_in[0], "out": w_out[0], "up": w_up[0], "bs": w_branch_ssm_2[0],
            "ba": w_branch_att_2[0], "out2": w_out_2[0]}
    wi2 = w_in_2[0]
    o = 0
    for name, width in (("z", 1024), ("xs", 1024), ("B", 512), ("C", 512), ("dt", 16), ("q", 1024),
                        ("k", 1024), ("v", 1024), ("f", 16), ("za", 1024), ("gs", 1024),
                        ("ga", 1024)):
        wmap[name] = wi2[:, o:o + width]
        o += width
    dtf = np.zeros((1024, 128), f)
    dtf[:, 0:16] = wmap["dt"]
    dtf[:, 32:48] = wmap["f"]
    wmap["dtf"] = dtf
    s = plan()
    wst = np.empty((len(s), 128, 1024), f)
    f0 = [sum(FG[:g]) for g in range(len(FG))]
    for i, (kind, name, n) in enumerate(s):
        if kind == "a":
            wst[i] = w_ada[0][n * 128:(n + 1) * 128, name * 1024:(name + 1) * 1024]
        elif name.startswith("down"):
            g = int(name[4:])
            nf = FG[g]
            w = 1024 // nf
            blk = w_down[0][f0[g] * 128:(f0[g] + nf) * 128, n * w:(n + 1) * w]
            wst[i] = blk.reshape(nf, 128, w).transpose(1, 0, 2).reshape(128, 1024)
        else:
            blk = wmap[name][:, n * 128:(n + 1) * 128].reshape(8, 128, 128)
            if name == "out":
                blk = np.concatenate([blk[4:], blk[:4]])
            wst[i] = blk.transpose(1, 0, 2).reshape(128, 1024)
    par = np.zeros((128, NPAR), f)

    def put(name, a):
        par[:, POFF[name]:POFF[name] + a.shape[1]] = a

    put("c", cols(c[0]))
    put("b_ada", cols(b_ada[0]))
    put("g1", cols(g_norm1[0]))
    put("g2", cols(g_norm2[0]))
    put("gf", cols(g_final))
    put("gpre", cols(pre_norm_g_2[0]))
    put("gpost", cols(post_norm_g_2[0]))
    put("gq", np.tile(g_q[0], 2)[:, None])
    put("gk", np.tile(g_k[0], 2)[:, None])
    put("gv", np.tile(g_tok_v[0], 2)[:, None])
    put("gao", cols(g_attn_out[0]))
    put("gto", cols(g_tok_out[0]))
    put("wc", np.concatenate([cols(w_conv[0][j]) for j in range(3)], 1))
    put("bc", cols(b_conv[0]))
    put("wc2", np.concatenate([cols(conv_w_2[0][j]) for j in range(4)], 1))
    put("bc2", cols(conv_b_2[0]))
    rowb = np.zeros((128, 1), f)
    rowb[0:16, 0] = dt_bias_2[0]
    rowb[32:48, 0] = fgate_b_2[0]
    put("rowb", rowb)
    rowa = np.zeros((128, 1), f)
    rowa[0:16, 0] = a_log_2[0]
    put("rowa", rowa)
    put("dskip", cols(np.repeat(d_skip_2[0], 64)))
    put("gssm", cols(ssm_norm_g_2[0]))
    bsb = np.repeat(np.asarray(b_s[0]).reshape(4, 2, 1, 128), 64, axis=2)
    bsb = bsb.reshape(4, 128, 128).transpose(1, 0, 2).reshape(128, 512)
    wsT = np.asarray(w_s[0]).transpose(2, 0, 1).reshape(128, 1024)
    cst, rope = constants()
    return {"wst": wst, "xT": np.ascontiguousarray(np.asarray(x[0]).T), "cst": cst, "par": par,
            "bsb": np.ascontiguousarray(bsb), "rope": rope, "wsT": np.ascontiguousarray(wsT)}


def constants():
    f = np.float32
    i = np.arange(128)
    cst = np.zeros((7, 128, 128), f)
    cst[0] = np.eye(128)
    cst[1] = 1.0
    cst[2] = (i[:, None] // 64 == i[None, :] // 64)
    for m in range(128):
        if m % 32 < 16:
            cst[3, m + 16, m] = -1.0
        else:
            cst[3, m - 16, m] = 1.0
    cst[4, 127, :] = 1.0
    cst[5] = (i[:, None] >= i[None, :])
    cst[6] = (i[:, None] <= i[None, :])
    cst = np.ascontiguousarray(cst.transpose(1, 0, 2).reshape(128, 896))
    t = np.arange(1024)
    inv = np.power(f(10000.0), -np.arange(0, 32, 2, dtype=f) / f(32)).astype(f)
    ar = ((t // 64).astype(f)[:, None] * inv[None, :]).astype(f)
    ac = ((t % 64).astype(f)[:, None] * inv[None, :]).astype(f)
    ang = np.concatenate([ar, ar, ac, ac], 1).T
    ang = np.concatenate([ang, ang], 0)
    rope = np.stack([np.cos(ang), np.sin(ang)]).astype(f)
    return cst, rope


def kernel(**inputs):
    import concourse.bacc as bacc
    from concourse.bass_utils import run_bass_kernel_spmd

    nc = bacc.Bacc("TRN2", target_bir_lowering=False, num_devices=1)
    arrays = layout(**{n: np.asarray(a) for n, a in inputs.items()})
    args = {n: nc.dram_tensor("in_" + n, a.shape, mybir.dt.from_np(a.dtype),
                              kind="ExternalInput").ap() for n, a in arrays.items()}
    out = nc.dram_tensor("out_0", (1024, 1024), F32, kind="ExternalOutput").ap()
    scratch = {n: nc.dram_tensor("scratch_" + n, s, F32, kind="Internal").ap()
               for n, s in SCRATCH.items()}
    build_program(nc, **args, out=out, scratch=scratch, phases=PHASES)
    r = run_bass_kernel_spmd(nc, [{"in_" + n: a for n, a in arrays.items()}], core_ids=[0])
    got = r.results[0]["out_0"]
    return np.ascontiguousarray(np.asarray(got).T)[None]
```
